# Optimizing a Trainium2 kernel written in Bass

```python
import jax
import jax.numpy as jnp
from jax import lax
import numpy as np
import math
import jax, jax.numpy as jnp

D_MODEL = 2048
BATCH = 1
SEQ = 256
DEPTH = 2

CHUNK = 64
N_MEM = 256
N_BRANCH = 4
BRANCH_WIDTH = D_MODEL // 4
HEAD_DIM = 128
N_HEADS = BRANCH_WIDTH // HEAD_DIM
IDX_HEADS = 8
IDX_DIM = 64
TOPK_MAX = 256
Q_BLOCK = 128
ROPE_BASE = 10000.0
EPS = 1e-6
W = BRANCH_WIDTH
SPLIT_SIZES = (W, W, W, W, IDX_HEADS * IDX_DIM, IDX_DIM, IDX_HEADS,
               W, W, W, W,
               W, W, W, W,
               W, W,
               N_BRANCH * D_MODEL)
IN_WIDTH = sum(SPLIT_SIZES)


def rms_norm(x, g):
    xf = x.astype(jnp.float32)
    y = xf * lax.rsqrt(jnp.mean(xf * xf, axis=-1, keepdims=True) + EPS)
    return (y * g.astype(jnp.float32)).astype(x.dtype)

def head_rms_norm(t, g):
    tf = t.astype(jnp.float32)
    y = tf * lax.rsqrt(jnp.mean(tf * tf, axis=-1, keepdims=True) + EPS)
    return (y * g.astype(jnp.float32)).astype(t.dtype)

def split_cols(u):
    parts = []
    off = 0
    for n in SPLIT_SIZES:
        parts.append(u[..., off:off + n])
        off += n
    return parts

def rope_tables(seq):
    inv = ROPE_BASE ** (-jnp.arange(0, HEAD_DIM, 2, dtype=jnp.float32) / HEAD_DIM)
    ang = jnp.arange(seq, dtype=jnp.float32)[:, None] * inv[None, :]
    return jnp.cos(ang), jnp.sin(ang)

def rope(t, cos, sin):
    half = HEAD_DIM // 2
    t1 = t[..., :half].astype(jnp.float32)
    t2 = t[..., half:].astype(jnp.float32)
    c, s = cos[:, None, :], sin[:, None, :]
    return jnp.concatenate([t1 * c - t2 * s, t1 * s + t2 * c], axis=-1).astype(t.dtype)

def sparse_index_attention(q, k, v, qi, ki, wi):
    B, S, H, Dh = q.shape
    n_sel = min(TOPK_MAX, S // 4)
    nb = S // Q_BLOCK
    key_chunk = jnp.arange(S) // CHUNK

    def to_blocks(t):
        return jnp.moveaxis(t.reshape(B, nb, Q_BLOCK, *t.shape[2:]), 1, 0)

    def block(args):
        start, qb, qib, wib = args
        q_chunk = (start + jnp.arange(Q_BLOCK)) // CHUNK
        visible = key_chunk[None, :] <= q_chunk[:, None]
        rel = jax.nn.relu(jnp.einsum('bqhd,bsd->bqhs', qib, ki).astype(jnp.float32) * IDX_DIM ** -0.5)
        score = jnp.einsum('bqh,bqhs->bqs', wib.astype(jnp.float32) * IDX_HEADS ** -0.5, rel)
        score = jnp.where(visible[None], score, -jnp.inf)
        _, sel = lax.top_k(score, n_sel)
        sel_ok = key_chunk[sel] <= q_chunk[None, :, None]
        ks = jax.vmap(lambda kk, ii: kk[ii])(k, sel)
        vs = jax.vmap(lambda vv, ii: vv[ii])(v, sel)
        logits = jnp.einsum('bqhd,bqkhd->bhqk', qb, ks).astype(jnp.float32) * HEAD_DIM ** -0.5
        logits = jnp.where(sel_ok[:, None], logits, -jnp.inf)
        p = jax.nn.softmax(logits, axis=-1).astype(vs.dtype)
        return jnp.einsum('bhqk,bqkhd->bqhd', p, vs)

    starts = jnp.arange(nb) * Q_BLOCK
    out = lax.map(block, (starts, to_blocks(q), to_blocks(qi), to_blocks(wi)))
    return jnp.moveaxis(out, 0, 1).reshape(B, S, H, Dh)

def retention(q, k, v):
    B, S, H, d = q.shape
    nc = S // CHUNK
    q = q.astype(jnp.float32).reshape(B, nc, CHUNK, H, d)
    k = k.astype(jnp.float32).reshape(B, nc, CHUNK, H, d)
    v = v.astype(jnp.float32).reshape(B, nc, CHUNK, H, d)
    log_g = jnp.log1p(-jnp.exp2(-5.0 - jnp.arange(H, dtype=jnp.float32)))
    pos = jnp.arange(CHUNK, dtype=jnp.float32)
    intra = jnp.exp(log_g[:, None, None] * jnp.abs(pos[:, None] - pos[None, :]))
    s = jnp.einsum('bnchd,bnehd->bnhce', q, k) * intra
    o_intra = jnp.einsum('bnhce,bnehd->bnchd', s, v)
    k_dec = k * jnp.exp(log_g[None, :] * (CHUNK - 1 - pos)[:, None])[:, :, None]
    kv = jnp.einsum('bnehd,bnehv->nbhdv', k_dec, v)
    chunk_decay = jnp.exp(log_g * CHUNK)[None, :, None, None]

    def step(state, kv_n):
        return chunk_decay * state + kv_n, state

    _, s_prev = lax.scan(step, jnp.zeros_like(kv[0]), kv)
    q_dec = q * jnp.exp(log_g[None, :] * (pos + 1.0)[:, None])[:, :, None]
    o_inter = jnp.einsum('bnchd,nbhdv->bnchv', q_dec, s_prev)
    return (o_intra + o_inter).reshape(B, S, H, d)

def hgrn2(f, i, q):
    B, S, H, d = q.shape
    nc = S // CHUNK
    f = f.astype(jnp.float32).reshape(B, nc, CHUNK, H, d)
    i = i.astype(jnp.float32).reshape(B, nc, CHUNK, H, d)
    q = q.astype(jnp.float32).reshape(B, nc, CHUNK, H, d)
    kin = 1.0 - f

    def tmaj(t):
        return jnp.moveaxis(t, 2, 0)

    def step(state, inp):
        f_t, k_t, i_t, q_t = inp
        state = f_t[..., None] * state + k_t[..., None] * i_t[..., None, :]
        return state, jnp.einsum('bnhd,bnhdv->bnhv', q_t, state)

    s0 = jnp.zeros((B, nc, H, d, d), jnp.float32)
    s_local, o_intra = lax.scan(step, s0, (tmaj(f), tmaj(kin), tmaj(i), tmaj(q)))
    o_intra = jnp.moveaxis(o_intra, 0, 2)
    cum = jnp.cumsum(jnp.log(f), axis=2)
    chunk_decay = jnp.exp(cum[:, :, -1])

    def cstep(state, inp):
        dec, sl = inp
        return dec[..., None] * state + sl, state

    _, s_prev = lax.scan(cstep, jnp.zeros((B, H, d, d), jnp.float32),
                         (jnp.moveaxis(chunk_decay, 1, 0), jnp.moveaxis(s_local, 1, 0)))
    o_inter = jnp.einsum('bnchd,nbhdv->bnchv', q * jnp.exp(cum), s_prev)
    return (o_intra + o_inter).reshape(B, S, H, d)

def memory_attention(q, mk, mv):
    logits = jnp.einsum('bshd,bmhd->bhsm', q, mk).astype(jnp.float32) * HEAD_DIM ** -0.5
    p = jax.nn.softmax(logits, axis=-1).astype(mv.dtype)
    return jnp.einsum('bhsm,bmhd->bshd', p, mv)

def hybrid_layer(x, mem, norm_g, w_in, qk_g, ret_g, hgrn_g, lb, w_mem_kv, w_branch, w_out, cos, sin):
    B, S, _ = x.shape
    dt = x.dtype
    h = rms_norm(x, norm_g)
    u = h @ w_in
    (a_q, a_k, a_v, a_z, a_qi, a_ki, a_wi,
     b_q, b_k, b_v, b_z,
     c_f, c_i, c_q, c_z,
     m_q, m_z, gates) = split_cols(u)

    def heads(t):
        return t.reshape(t.shape[0], t.shape[1], N_HEADS, HEAD_DIM)

    y_a = sparse_index_attention(head_rms_norm(heads(a_q), qk_g[0]), head_rms_norm(heads(a_k), qk_g[1]),
                                 heads(a_v), a_qi.reshape(B, S, IDX_HEADS, IDX_DIM), a_ki, a_wi)
    y_b = retention(rope(heads(b_q), cos, sin), rope(heads(b_k), cos, sin) * HEAD_DIM ** -0.5, heads(b_v))
    y_b = head_rms_norm(y_b, ret_g)
    f = lb + (1.0 - lb) * jax.nn.sigmoid(heads(c_f).astype(jnp.float32))
    y_c = head_rms_norm(hgrn2(f, heads(c_i), heads(c_q)), hgrn_g)
    mkv = mem @ w_mem_kv
    m_k, m_v = mkv[..., :W], mkv[..., W:]
    y_m = memory_attention(head_rms_norm(heads(m_q), qk_g[2]), head_rms_norm(heads(m_k), qk_g[3]), heads(m_v))

    gate_all = gates.reshape(B, S, N_BRANCH, D_MODEL)
    merged = jnp.zeros_like(x)
    for n, (y, z) in enumerate(((y_a, a_z), (y_b, b_z), (y_c, c_z), (y_m, m_z))):
        branch = y.reshape(B, S, W).astype(dt) * jax.nn.silu(z)
        merged = merged + jax.nn.sigmoid(gate_all[:, :, n]) * (branch @ w_branch[n])
    return x + merged @ w_out

def first_inputs(seed: int = 0) -> dict:
    key = jax.random.key(seed)
    ks = jax.random.split(key, 12)
    x = jax.random.normal(ks[0], (BATCH, SEQ, D_MODEL), jnp.float32)
    mem = jax.random.normal(ks[1], (BATCH, N_MEM, D_MODEL), jnp.float32)
    norm_g = 1.0 + 0.02 * jax.random.normal(ks[2], (DEPTH, D_MODEL), jnp.float32)
    w_in = jax.random.normal(ks[3], (DEPTH, D_MODEL, IN_WIDTH), jnp.float32) * D_MODEL ** -0.5
    qk_norm_g = 1.0 + 0.02 * jax.random.normal(ks[4], (DEPTH, 4, HEAD_DIM), jnp.float32)
    ret_norm_g = 1.0 + 0.02 * jax.random.normal(ks[5], (DEPTH, N_HEADS, HEAD_DIM), jnp.float32)
    hgrn_norm_g = 1.0 + 0.02 * jax.random.normal(ks[6], (DEPTH, N_HEADS, HEAD_DIM), jnp.float32)
    lb_logits = 0.5 * jax.random.normal(ks[7], (DEPTH, N_HEADS, HEAD_DIM), jnp.float32)
    w_mem_kv = jax.random.normal(ks[8], (DEPTH, D_MODEL, 2 * W), jnp.float32) * D_MODEL ** -0.5
    w_branch = jax.random.normal(ks[9], (DEPTH, N_BRANCH, W, D_MODEL), jnp.float32) * W ** -0.5
    w_out = jax.random.normal(ks[10], (DEPTH, D_MODEL, D_MODEL), jnp.float32) * D_MODEL ** -0.5
    return {'x': x, 'mem': mem, 'norm_g': norm_g, 'w_in': w_in, 'qk_norm_g': qk_norm_g,
            'ret_norm_g': ret_norm_g, 'hgrn_norm_g': hgrn_norm_g, 'lb_logits': lb_logits,
            'w_mem_kv': w_mem_kv, 'w_branch': w_branch, 'w_out': w_out}

def first_block(x, mem, norm_g, w_in, qk_norm_g, ret_norm_g, hgrn_norm_g, lb_logits, w_mem_kv, w_branch, w_out):
    seq = x.shape[1]
    p = jax.nn.softmax(lb_logits.astype(jnp.float32), axis=0)
    lower_bounds = jnp.cumsum(p, axis=0) - p[0:1]
    cos, sin = rope_tables(seq)
    for l in range(DEPTH):
        x = hybrid_layer(x, mem, norm_g[l], w_in[l], qk_norm_g[l], ret_norm_g[l], hgrn_norm_g[l],
                         lower_bounds[l], w_mem_kv[l], w_branch[l], w_out[l], cos, sin)
    return x


DEPTH_2 = 1

MLA_HEADS = 8
Q_LORA = 512
KV_LORA = 512
QK_NOPE = 128
QK_ROPE = 64
V_DIM = 128
ROPE_THETA = 10000.0
DIL_HEADS = 8
DIL_DIM = 128
DIL_PATTERNS = ((128, 1), (512, 4), (2048, 16))
DIL_BLOCK = 64
N_BRANCH_2 = 2
D_FF = -(-8 * D_MODEL // (3 * 256)) * 256
RMS_EPS = 1e-6
NEG_INF = -1e30
D_IN = Q_LORA + KV_LORA + QK_ROPE + 3 * DIL_HEADS * DIL_DIM + N_BRANCH_2 * D_MODEL


def rms_norm_2(x, g):
    xf = x.astype(jnp.float32)
    y = xf * lax.rsqrt(jnp.mean(xf * xf, axis=-1, keepdims=True) + RMS_EPS)
    return (y * g.astype(jnp.float32)).astype(x.dtype)

def rope_tables_2(seq):
    inv = ROPE_THETA ** (-jnp.arange(0, QK_ROPE, 2, dtype=jnp.float32) / QK_ROPE)
    ang = jnp.arange(seq, dtype=jnp.float32)[:, None] * inv[None, :]
    return jnp.cos(ang), jnp.sin(ang)

def apply_rope(x, cos, sin):
    x1, x2 = jnp.split(x, 2, axis=-1)
    c = cos.astype(x.dtype)
    s = sin.astype(x.dtype)
    return jnp.concatenate([x1 * c - x2 * s, x1 * s + x2 * c], axis=-1)

def alibi_slopes(n_heads):
    return jnp.power(2.0, -8.0 * jnp.arange(1, n_heads + 1, dtype=jnp.float32) / n_heads)

def mla_attention(q_nope, q_rope, k_nope, k_rope, v):
    B, S, H, _ = q_nope.shape
    nq = S // Q_BLOCK
    scale = (QK_NOPE + QK_ROPE) ** -0.5

    def to_blocks(t):
        return jnp.moveaxis(t.reshape(B, nq, Q_BLOCK, *t.shape[2:]), 1, 0)

    def attend(blk):
        qn, qr = blk
        s = (jnp.einsum('bqhd,bkhd->bhqk', qn, k_nope, preferred_element_type=jnp.float32)
             + jnp.einsum('bqhd,bkd->bhqk', qr, k_rope, preferred_element_type=jnp.float32)) * scale
        p = jax.nn.softmax(s, axis=-1).astype(v.dtype)
        return jnp.einsum('bhqk,bkhd->bqhd', p, v)

    o = lax.map(attend, (to_blocks(q_nope), to_blocks(q_rope)))
    return jnp.moveaxis(o, 0, 1).reshape(B, S, H, v.shape[-1])

def strided_band_attention(q, k, v, slopes, n_side, dil):
    B, S, H, D = q.shape
    L = S // dil
    nb = -(-L // DIL_BLOCK)
    Lp = nb * DIL_BLOCK

    def to_sub(t):
        return t.reshape(B, L, dil, H, D).transpose(0, 2, 1, 3, 4)

    qs = jnp.pad(to_sub(q), ((0, 0), (0, 0), (0, Lp - L), (0, 0), (0, 0)))
    qs = qs.reshape(B, dil, nb, DIL_BLOCK, H, D)

    def windows(t):
        tp = jnp.pad(to_sub(t), ((0, 0), (0, 0), (DIL_BLOCK, DIL_BLOCK + Lp - L), (0, 0), (0, 0)))
        tb = tp.reshape(B, dil, nb + 2, DIL_BLOCK, H, D)
        return jnp.concatenate([tb[:, :, :-2], tb[:, :, 1:-1], tb[:, :, 2:]], axis=3)

    kw = windows(k)
    vw = windows(v)

    qi = jnp.arange(DIL_BLOCK)[:, None]
    kj = jnp.arange(3 * DIL_BLOCK)[None, :]
    delta = kj - DIL_BLOCK - qi
    kpos = (jnp.arange(nb)[:, None] - 1) * DIL_BLOCK + jnp.arange(3 * DIL_BLOCK)[None, :]
    valid = (jnp.abs(delta) <= n_side)[None] & ((kpos >= 0) & (kpos < L))[:, None, :]
    bias = -slopes[:, None, None] * (dil * jnp.abs(delta)).astype(jnp.float32)[None]

    s = jnp.einsum('bcnqhd,bcnkhd->bcnhqk', qs, kw, preferred_element_type=jnp.float32) * (D ** -0.5)
    s = jnp.where(valid[:, None], s + bias, NEG_INF)
    m = jnp.max(s, axis=-1, keepdims=True)
    p = jnp.exp(s - m)
    l = jnp.sum(p, axis=-1)
    o = jnp.einsum('bcnhqk,bcnkhd->bcnqhd', p.astype(v.dtype), vw).astype(jnp.float32)
    o = o / jnp.swapaxes(l, -1, -2)[..., None]
    lse = jnp.swapaxes(m[..., 0] + jnp.log(l), -1, -2)

    o = o.reshape(B, dil, Lp, H, D)[:, :, :L].transpose(0, 2, 1, 3, 4).reshape(B, S, H, D)
    lse = lse.reshape(B, dil, Lp, H)[:, :, :L].transpose(0, 2, 1, 3).reshape(B, S, H)
    return o, lse

def dilated_attention(q, k, v):
    slopes = alibi_slopes(q.shape[2])
    outs, lses = [], []
    for window, dil in DIL_PATTERNS:
        o, lse = strided_band_attention(q, k, v, slopes, window // (2 * dil), dil)
        outs.append(o)
        lses.append(lse)
    w = jax.nn.softmax(jnp.stack(lses), axis=0)
    o = sum(w[g][..., None] * outs[g] for g in range(len(DIL_PATTERNS)))
    return o.astype(v.dtype)

def hybrid_layer_2(x, cos, sin, g_mix, w_in, b_gate, g_cq, w_uq, g_ckv, w_ukv,
                 g_q_nope, g_q_rope, g_k_nope, g_k_rope, g_q_dil, g_k_dil,
                 w_o_mla, w_o_dil, w_o, g_ffn, w_gate_up, w_down):
    B, S, _ = x.shape
    h = rms_norm_2(x, g_mix)
    proj = h @ w_in
    dh = DIL_HEADS * DIL_DIM
    cuts = np.cumsum([Q_LORA, KV_LORA, QK_ROPE, dh, dh, dh]).tolist()
    c_q, c_kv, k_r, q_d, k_d, v_d, gate = jnp.split(proj, cuts, axis=-1)

    q = (rms_norm_2(c_q, g_cq) @ w_uq).reshape(B, S, MLA_HEADS, QK_NOPE + QK_ROPE)
    q_nope, q_rope = jnp.split(q, [QK_NOPE], axis=-1)
    q_nope = rms_norm_2(q_nope, g_q_nope)
    q_rope = apply_rope(rms_norm_2(q_rope, g_q_rope), cos[:, None, :], sin[:, None, :])
    kv = (rms_norm_2(c_kv, g_ckv) @ w_ukv).reshape(B, S, MLA_HEADS, QK_NOPE + V_DIM)
    k_nope, v_a = jnp.split(kv, [QK_NOPE], axis=-1)
    k_nope = rms_norm_2(k_nope, g_k_nope)
    k_rope = apply_rope(rms_norm_2(k_r, g_k_rope), cos, sin)
    o_a = mla_attention(q_nope, q_rope, k_nope, k_rope, v_a)
    y_a = o_a.reshape(B, S, MLA_HEADS * V_DIM) @ w_o_mla

    qd = rms_norm_2(q_d.reshape(B, S, DIL_HEADS, DIL_DIM), g_q_dil)
    kd = rms_norm_2(k_d.reshape(B, S, DIL_HEADS, DIL_DIM), g_k_dil)
    vd = v_d.reshape(B, S, DIL_HEADS, DIL_DIM)
    o_b = dilated_attention(qd, kd, vd)
    y_b = o_b.reshape(B, S, dh) @ w_o_dil

    g = jax.nn.sigmoid((gate + b_gate).astype(jnp.float32)).astype(x.dtype)
    g = g.reshape(B, S, N_BRANCH_2, D_MODEL)
    x = x + (g[:, :, 0] * y_a + g[:, :, 1] * y_b) @ w_o

    gt, up = jnp.split(rms_norm_2(x, g_ffn) @ w_gate_up, 2, axis=-1)
    return x + (jax.nn.silu(gt) * up) @ w_down

def second_inputs(seed: int = 0) -> dict:
    key = jax.random.key(seed)
    ks = jax.random.split(key, 22)

    def dense(k, fan_in, fan_out):
        return jax.random.normal(k, (DEPTH_2, fan_in, fan_out), jnp.float32) * fan_in ** -0.5

    def gain(k, n):
        return 1.0 + 0.05 * jax.random.normal(k, (DEPTH_2, n), jnp.float32)

    return {
        "x": jax.random.normal(ks[0], (BATCH, SEQ, D_MODEL), jnp.float32),
        "g_mix": gain(ks[1], D_MODEL),
        "w_in": dense(ks[2], D_MODEL, D_IN),
        "b_gate": 0.02 * jax.random.normal(ks[3], (DEPTH_2, N_BRANCH_2 * D_MODEL), jnp.float32),
        "g_cq": gain(ks[4], Q_LORA),
        "w_uq": dense(ks[5], Q_LORA, MLA_HEADS * (QK_NOPE + QK_ROPE)),
        "g_ckv": gain(ks[6], KV_LORA),
        "w_ukv": dense(ks[7], KV_LORA, MLA_HEADS * (QK_NOPE + V_DIM)),
        "g_q_nope": gain(ks[8], QK_NOPE),
        "g_q_rope": gain(ks[9], QK_ROPE),
        "g_k_nope": gain(ks[10], QK_NOPE),
        "g_k_rope": gain(ks[11], QK_ROPE),
        "g_q_dil": gain(ks[12], DIL_DIM),
        "g_k_dil": gain(ks[13], DIL_DIM),
        "w_o_mla": dense(ks[14], MLA_HEADS * V_DIM, D_MODEL),
        "w_o_dil": dense(ks[15], DIL_HEADS * DIL_DIM, D_MODEL),
        "w_o": dense(ks[16], D_MODEL, D_MODEL),
        "g_ffn": gain(ks[17], D_MODEL),
        "w_gate_up": dense(ks[18], D_MODEL, 2 * D_FF),
        "w_down": dense(ks[19], D_FF, D_MODEL),
    }

def second_block(x, g_mix, w_in, b_gate, g_cq, w_uq, g_ckv, w_ukv,
              g_q_nope, g_q_rope, g_k_nope, g_k_rope, g_q_dil, g_k_dil,
              w_o_mla, w_o_dil, w_o, g_ffn, w_gate_up, w_down):
    cos, sin = rope_tables_2(x.shape[1])
    for i in range(DEPTH_2):
        x = hybrid_layer_2(x, cos, sin, g_mix[i], w_in[i], b_gate[i], g_cq[i], w_uq[i],
                         g_ckv[i], w_ukv[i], g_q_nope[i], g_q_rope[i], g_k_nope[i],
                         g_k_rope[i], g_q_dil[i], g_k_dil[i], w_o_mla[i], w_o_dil[i],
                         w_o[i], g_ffn[i], w_gate_up[i], w_down[i])
    return x


def setup_inputs(seed=0):
    out = dict(first_inputs(seed))
    for name, value in second_inputs(seed + 1).items():
        if name != "x":
            out[name + "_2"] = value
    return out


def reference(
    x, mem, norm_g, w_in, qk_norm_g, ret_norm_g, hgrn_norm_g, lb_logits, w_mem_kv, w_branch,
    w_out, g_mix_2, w_in_2, b_gate_2, g_cq_2, w_uq_2, g_ckv_2, w_ukv_2, g_q_nope_2, g_q_rope_2,
    g_k_nope_2, g_k_rope_2, g_q_dil_2, g_k_dil_2, w_o_mla_2, w_o_dil_2, w_o_2, g_ffn_2,
    w_gate_up_2, w_down_2,
):
    x = first_block(
        x, mem, norm_g, w_in, qk_norm_g, ret_norm_g, hgrn_norm_g, lb_logits, w_mem_kv, w_branch,
        w_out,
    )
    return second_block(
        x, g_mix_2, w_in_2, b_gate_2, g_cq_2, w_uq_2, g_ckv_2, w_ukv_2, g_q_nope_2, g_q_rope_2,
        g_k_nope_2, g_k_rope_2, g_q_dil_2, g_k_dil_2, w_o_mla_2, w_o_dil_2, w_o_2, g_ffn_2,
        w_gate_up_2, w_down_2,
    )


_drawn_inputs = setup_inputs


def setup_inputs(seed=0):
    import zlib

    import numpy as np

    out = dict(_drawn_inputs(seed))
    spreads = {}
    factors = {'qk_norm_g': 8.0,
     'ret_norm_g': 4.703,
     'hgrn_norm_g': 5.03,
     'g_mix_2': 4.705,
     'b_gate_2': 8.0,
     'g_cq_2': 8.0,
     'g_ckv_2': 8.0,
     'g_q_nope_2': 8.0,
     'g_q_rope_2': 8.0,
     'g_k_nope_2': 8.0,
     'g_k_rope_2': 8.0,
     'g_q_dil_2': 8.0,
     'g_k_dil_2': 8.0,
     'g_ffn_2': 8.0}
    for name, (base, spread) in spreads.items():
        noise = np.random.default_rng([zlib.crc32(name.encode()), seed]).standard_normal(out[name].shape)
        drawn = base * np.exp(spread * noise) if base else spread * noise
        out[name] = jnp.asarray(drawn.astype(out[name].dtype))
    for name, factor in factors.items():
        out[name] = (out[name] * factor).astype(out[name].dtype)
    return out
```

```python
from contextlib import ExitStack

import numpy as np

import concourse.bass as bass
from concourse import mybir

F32 = mybir.dt.float32
F32R = mybir.dt.float32r
U8 = mybir.dt.uint8
ALU = mybir.AluOpType
ACT = mybir.ActivationFunctionType
AX = mybir.AxisListType.X

P = 128
D = 2048
T = 256
TT = T // P
W = 512
H = 4
HD = 128
DEPTH = 2
CHUNK = 64
N_SEL = T // 4
IDX_HEADS = 8
IDX_DIM = 64
EPS = 1e-6
KD = D // P
NB = 512
CK = 2
RING = 4
N_FF = 5632 // NB
BIG = 1e30

A0, B0, C0, M0, G0 = 0, 2632, 4680, 6728, 7752
IN_BLOCKS = [
    ("c_f", C0, NB, "copy"), ("c_i", C0 + 512, NB, "copy"), ("c_q", C0 + 1024, NB, "copy"), ("c_z", C0 + 1536, NB, "silu"),
    ("a_q", A0, NB, "copy"), ("a_k", A0 + 512, NB, "copy"), ("a_v", A0 + 1024, NB, "copy"), ("a_z", A0 + 1536, NB, "silu"),
    ("a_qi", A0 + 2048, NB, "copy"), ("a_kw", A0 + 2560, IDX_DIM + IDX_HEADS, "copy"),
    ("m_q", M0, NB, "copy"), ("m_z", M0 + 512, NB, "silu"),
    ("b_q", B0, NB, "copy"), ("b_k", B0 + 512, NB, "copy"), ("b_v", B0 + 1024, NB, "copy"), ("b_z", B0 + 1536, NB, "silu"),
]
BRANCHES = "camb"
BRANCH_ROW = {"a": 0, "b": 1, "c": 2, "m": 3}
IN2_BLOCKS = [
    ("cq", 0, NB, "copy"), ("ckv", 512, NB, "copy"), ("kr", 1024, 64, "copy"),
    ("qd0", 1088, NB, "copy"), ("qd1", 1600, NB, "copy"), ("kd0", 2112, NB, "copy"), ("kd1", 2624, NB, "copy"),
    ("vd0", 3136, NB, "copy"), ("vd1", 3648, NB, "copy"),
]
G2 = 4160
UQ_BLOCKS = [(f"uq{i}", i * NB, NB, "copy") for i in range(3)]
UKV_BLOCKS = [(f"ukv{i}", i * NB, NB, "copy") for i in range(4)]
HEADS2 = 8
NOPE, ROPE2 = 128, 64
QW = NOPE + ROPE2

PRO_BLOCKS = 2 * DEPTH
LAYER_BLOCKS = len(IN_BLOCKS) + 8 * 4 + 4
LAYER_CHUNKS = 8 * len(IN_BLOCKS) + 40 * 4 + 32
LAYER_BLOCK = {b[0]: PRO_BLOCKS + i for i, b in enumerate(IN_BLOCKS)}
LAST0 = PRO_BLOCKS + DEPTH * LAYER_BLOCKS
LAST_BLOCK = {b[0]: LAST0 + i for i, b in enumerate(IN2_BLOCKS + UQ_BLOCKS + UKV_BLOCKS)}

HALVES = [1 << i for i in range(7)]
LEVELS = 1 + len(HALVES)

CHAIN = {"dve": 70, "pool": 22}

C_PHASES = 2 * (2 + LEVELS + 1 + 4)
AM_PHASES = (2 + 1 + IDX_HEADS // 2 + TT * IDX_HEADS // 2 + 8 + 5 * H) + (2 + 5 * H)
LAYER_PART = 36


def constants():
    t = np.arange(T)
    c = {}
    c["ident"] = np.eye(P, dtype=np.float32)
    log_g = np.log1p(-np.exp2(-5.0 - np.arange(H, dtype=np.float64)))
    vis = (t[:, None] // CHUNK) <= (t[None, :] // CHUNK)
    dist = np.abs(t[:, None] - t[None, :])
    ret = np.exp(log_g[:, None, None] * dist[None]) * vis[None] * HD ** -0.5
    c["ret"] = ret.reshape(H, TT, P, T).transpose(2, 0, 1, 3).reshape(P, H * TT * T).astype(np.float32)
    s, q = np.arange(P)[:, None], np.arange(P)[None, :]
    m = [s == q] + [((s // (2 * h)) == (q // (2 * h))) & (s % (2 * h) < h) & (q % (2 * h) >= h) for h in HALVES]
    c["levels"] = np.stack(m, 1).reshape(P, LEVELS * P).astype(np.float32)
    seen = (t[None, :] // CHUNK) <= (t[:, None] // CHUNK)
    c["seen"] = np.where(seen, 0.0, -BIG).reshape(TT, P, T).transpose(1, 0, 2).reshape(P, TT * T).astype(np.float32)

    def angles(dim):
        inv = np.float32(10000.0) ** (-np.arange(0, dim, 2, dtype=np.float32) / np.float32(dim))
        a = (t.astype(np.float32)[:, None] * inv[None, :].astype(np.float32)).astype(np.float64)
        return [f(a).reshape(TT, P, dim // 2).transpose(1, 0, 2).reshape(P, TT * dim // 2).astype(np.float32) for f in (np.cos, np.sin)]

    c["cos"], c["sin"] = angles(HD)
    c["cos2"], c["sin2"] = angles(ROPE2)
    count = sum(((dist % dil == 0) & (dist <= dil * (win // (2 * dil)))).astype(np.float64) for win, dil in ((128, 1), (512, 4), (2048, 16)))
    logc = np.where(count > 0, np.log(np.maximum(count, 1)), -BIG)
    c["dil"] = np.concatenate([x.reshape(TT, P, T).transpose(1, 0, 2).reshape(P, TT * T) for x in (-dist.astype(np.float64), logc)], 1).astype(np.float32)
    return c


class Tally:

    def __init__(self, unit=1, start=0):
        self.unit, self.k, self.rounds = unit, start, None

    def take(self):
        self.k += 1
        return self.k - 1

    def value(self, k):
        return k if self.rounds is None else self.rounds * self.unit + k

    def round_value(self, k, by=1):
        n = (k // self.unit) * by
        return n if self.rounds is None else self.rounds * by + n


def repeat(eng, n, tallies, body, name=None):
    with eng.Fori(0, n) as i:
        kept = []
        for t, step in tallies:
            assert step % t.unit == 0, (step, t.unit)
            kept.append((t, step, t.k, t.rounds))
            add = i * (step // t.unit)
            t.rounds = add if t.rounds is None else t.rounds + add
        body(i)
        for t, step, k, rounds in kept:
            assert t.k - k == step, (name, t.k - k, step)
            t.rounds = rounds
            t.k = k + n * step


def hybrid_program(nc, x, mem, norm_g, w_in, qk_g, ret_g, hgrn_g, lb_logits, w_mem_kv, w_branch, w_out,
                   g_mix, w_in2, b_gate, g_cq, w_uq, g_ckv, w_ukv, g_qn, g_qr, g_kn, g_kr, g_qd, g_kd,
                   w_o_mla, w_o_dil, w_o2, g_ffn, w_gu, w_down,
                   k_ident, k_ret, k_levels, k_seen, k_cos, k_sin, k_cos2, k_sin2, k_dil, x_kept, mkv_kept, out):
    with ExitStack() as ctx:
        def sb(name, shape, dt=F32):
            return ctx.enter_context(nc.sbuf_tensor(name, shape, dt))

        def psum(name):
            return ctx.enter_context(nc.psum_tensor(name, [P, 512], F32))

        def sem(name):
            return ctx.enter_context(nc.semaphore(name))

        raw = sb("raw", [P, RING, CK, NB])
        w_hi = sb("w_hi", [P, RING, CK, NB], F32R)
        w_lo = sb("w_lo", [P, RING, CK, NB], F32R)
        xh = sb("xh", [P, KD, T], F32R)
        xl = sb("xl", [P, KD, T], F32R)
        yh = sb("yh", [P, KD, T], F32R)
        yl = sb("yl", [P, KD, T], F32R)
        arena = sb("arena", [P, 13456])
        tmp = sb("tmp", [P, 4352])
        core = sb("core", [P, 2048])
        yz = sb("yz", [P, 2, TT, P])
        stat = sb("stat", [P, 192])
        ident = sb("ident", [P, P])
        ret_tab = sb("ret_tab", [P, H * TT * T])
        levels = sb("levels", [P, LEVELS, P], U8)
        seen = sb("seen", [P, TT, T])
        cos = sb("cos", [P, TT, 64])
        sin = sb("sin", [P, TT, 64])
        par_l = sb("par_l", [P, DEPTH, LAYER_PART])
        par = sb("par", [P, 96])
        k2 = sb("k2", [P, 2, TT, 32])
        g2 = sb("g2", [P, 2, ROPE2])

        def area(a, n, width):
            return arena[:, a:a + TT * width].rearrange("p (t n) -> p t n", t=TT)

        X, Q0, R0, M_0 = 0, 4096, 9360, 11408
        xs = area(X, 0, D)
        xn = area(Q0, 0, D)
        merged = xn
        u = {n: area(X + 1024 * i, 0, NB) for i, n in enumerate(("c_f", "c_i", "c_q", "c_z"))}
        u |= {n: area(X + 1024 * i, 0, NB) for i, n in enumerate(("b_q", "b_k", "b_v", "b_z"))}
        u |= {n: area(Q0 + 1024 * i, 0, NB) for i, n in enumerate(("a_q", "a_k", "a_v", "a_z", "a_qi"))}
        u["a_kw"] = area(Q0 + 5120, 0, IDX_DIM + IDX_HEADS)
        u |= {"m_q": area(R0, 0, NB), "m_z": area(R0 + 1024, 0, NB)}
        mk, mv = area(M_0, 0, NB), area(M_0 + 1024, 0, NB)
        qd, kd, vd = (area(2048 * i, 0, 1024) for i in range(3))
        q2, kv2 = area(6144, 0, 1536), area(9216, 0, 2048)
        cqn, ckvn = area(R0, 0, NB), area(R0 + 1024, 0, NB)
        krn = area(R0 + 4096 - 128, 0, 64)
        for i in range(2):
            u[f"qd{i}"], u[f"kd{i}"], u[f"vd{i}"] = (z[:, :, i * NB:(i + 1) * NB] for z in (qd, kd, vd))
        for i in range(3):
            u[f"uq{i}"] = q2[:, :, i * NB:(i + 1) * NB]
        for i in range(4):
            u[f"ukv{i}"] = kv2[:, :, i * NB:(i + 1) * NB]
        u |= {"cq": cqn, "ckv": ckvn, "kr": krn}
        bias_rows = arena[:, R0:R0 + 4096]
        hidden = area(R0, 0, NB)

        f2, q_c = tmp[:, 0:512], tmp[:, 512:1024]
        qp = [tmp[:, 1024 + 512 * i:1536 + 512 * i] for i in range(2)]
        ks = [tmp[:, 2048 + 512 * i:2560 + 512 * i] for i in range(2)]
        acc = tmp[:, 3072:3584]
        acc_off = tmp[:, 3584:3840]
        prod = [f2]
        at = 3840
        for i in range(7):
            n = 512 >> (i + 1)
            prod.append(tmp[:, at:at + n])
            at += n
        assert at <= 4352
        qi_t = tmp[0:IDX_DIM, 0:2048].rearrange("p (h t) -> p h t", h=IDX_HEADS)
        ki_t = tmp[0:IDX_DIM, 2048:2304]
        rel = [tmp[:, 2304 + 512 * i:2816 + 512 * i] for i in range(2)]
        score = tmp[:, 3328:3840].rearrange("p (t s) -> p t s", t=TT)
        squares = tmp[:, 0:1024]
        rope_t = [tmp[:, 512 * i:512 * i + 512] for i in range(3)]
        sig = tmp[:, 2048:3072].rearrange("p (t n) -> p t n", t=TT)
        kr_t = tmp[0:ROPE2, 3840:4096]
        qr_t = tmp[0:ROPE2, 4096:4352]
        rope2_tab = tmp[:, 3072:3584].rearrange("p (q k t n) -> p q k t n", q=2, k=4, t=TT)
        qk_t = core[:, 0:512]
        sc = core[:, 512:1024].rearrange("p (t s) -> p t s", t=TT)
        pr = core[:, 1024:1536].rearrange("p (t s) -> p t s", t=TT)
        p_t = core[:, 1536:2048].rearrange("p (s t) -> p s t", s=TT)

        ssq, rs = stat[:, 0:16], stat[:, 16:32]
        o_ssq, o_rs = stat[:, 32:34], stat[:, 34:36]
        x_ssq, x_rs = stat[:, 36:40], stat[:, 156:160]
        mx, nmx, esum, r_e = (stat[:, 40 + 2 * i:42 + 2 * i] for i in range(4))
        half = stat[:, 48:64]
        top8 = stat[:, 64:80]
        wis = stat[:, 80:96].rearrange("p (t h) -> p t h", t=TT)

        now = par[:, 0:LAYER_PART]
        x_gain, qk_gain, ret_gain, hg_gain, lb, oml = (now[:, i:j] for i, j in ((0, 16), (16, 20), (20, 24), (24, 28), (28, 32), (32, 36)))
        p_mix, p_ffn = par[:, 36:52], par[:, 52:68]
        p_cq, p_ckv = par[:, 68:72], par[:, 72:76]
        p_h2 = par[:, 76:80]
        lg = stat[:, 132:140].rearrange("p (l h) -> p l h", l=DEPTH)
        le = stat[:, 140:148].rearrange("p (l h) -> p l h", l=DEPTH)
        lt = stat[:, 148:156].rearrange("p (l h) -> p l h", l=2)

        G = [ctx.enter_context(nc.psum_tensor(f"G{i}", [P, TT, NB], F32)) for i in range(2)]
        PT = [psum(f"PT{i}") for i in range(2)]
        PS = psum("PS")
        PO = psum("PO")

        raw_landed = [sem(f"raw_landed{i}") for i in range(RING)]
        hi_done, lo_done, mm_done = sem("hi_done"), sem("lo_done"), sem("mm_done")
        gm_free = [sem(f"gm_free{i}") for i in range(2)]
        pt_full, pt_hi = sem("pt_full"), sem("pt_hi")
        pt_free = [sem(f"pt_free{i}") for i in range(2)]
        ps_full, ps_free = sem("ps_full"), sem("ps_free")
        po_full = sem("po_full")
        sig_done, sig_used = sem("sig_done"), sem("sig_used")
        x_sq_done, x_rs_done, xn_done = sem("x_sq_done"), sem("x_rs_done"), sem("xn_done")
        heads_squared, heads_summed, heads_normed = sem("heads_squared"), sem("heads_summed"), sem("heads_normed")
        max_done, exp_done = sem("max_done"), sem("exp_done")
        o_squared, o_scaled, y_ready = sem("o_squared"), sem("o_scaled"), sem("y_ready")
        gates_ready, ks_ready, qp_ready, acc_ready = sem("gates_ready"), sem("ks_ready"), sem("qp_ready"), sem("acc_ready")
        idx_ready, rel_used = sem("idx_ready"), sem("rel_used")
        roped = sem("roped")
        consts_in, pars_in, mem_in, x_in, x_out, x_back = (sem(n) for n in ("consts_in", "pars_in", "mem_in", "x_in", "x_out", "x_back"))
        x_ready, decayed = sem("x_ready"), sem("decayed")
        lb_shifted, lb_exp, pars_now = sem("lb_shifted"), sem("lb_exp"), sem("pars_now")
        mkv_out, mkv_in, bias_in, dil_in, all_out = (sem(n) for n in ("mkv_out", "mkv_in", "bias_in", "dil_in", "all_out"))
        rope2_ready = sem("rope2_ready")
        act_chain, dve_chain, pool_chain = sem("act_chain"), sem("dve_chain"), sem("pool_chain")
        ffn_ready = sem("ffn_ready")
        passed = sem("passed")

        def hold(eng, s, value):
            eng.wait_ge(s, value)
            eng.sem_inc(passed, 1)

        def plain(eng, s, value):
            eng.wait_ge(s, value)

        def turns_read(eng, tally, i, both=True, wait=plain):
            for n in ((i - 1, i) if both else (i,)):
                wait(eng, pt_free[n % 2], tally.round_value(n) + 1)

        def cut(w):
            return w.rearrange("(c j p) n -> c p j n", j=CK, p=P)

        v_in = cut(w_in.rearrange("l k n -> (l k) n"))
        v_mem = cut(w_mem_kv.rearrange("l k n -> (l k) n"))
        v_br = cut(w_branch.rearrange("l b k n -> (l b k) n"))
        v_out = cut(w_out.rearrange("l k n -> (l k) n"))
        v_in2, v_uq, v_ukv = cut(w_in2[0]), cut(w_uq[0]), cut(w_ukv[0])
        v_mla, v_dil, v_o2, v_gu, v_down = cut(w_o_mla[0]), cut(w_o_dil[0]), cut(w_o2[0]), cut(w_gu[0]), cut(w_down[0])

        rows = lambda a: a.rearrange("(t p) n -> p t n", p=P)

        PT_C = 8 + (2 * 2 + 4)
        PT_ATT = PT_C + (2 + 4 + 3 * H) + 3 * H + 2 * H
        PT_LAYER = PT_ATT + 8
        PS_C = 2 * (LEVELS + 1)
        PS_SEL = PS_C + TT * IDX_HEADS // 2
        PS_LAYER = PS_SEL + 3 * H
        PT_LAST = KD // 2 + DEPTH * PT_LAYER + 8 + 4 + 3 * HEADS2 + 1 + 4 * HEADS2

        def phases_after(y):
            if 38 <= y < 38 + C_PHASES:
                return 1
            if 85 <= y < 85 + (AM_PHASES + 1) // 2:
                return min(2, AM_PHASES - 2 * (y - 85))
            return 0

        def ks_buf(l):
            return ks[max(l - 1, 0) % 2]

        def qp_buf(l):
            return qp[(l - 1) % 2] if l else q_c

        block = ctx.enter_context(nc.Block())

        @block.sync
        def _(sp):
            at = Tally(RING)

            def load(view, width=NB):
                c = at.take()
                if c >= RING:
                    hold(sp, lo_done, at.value(c - RING + 1))
                sp.dma_start(raw[:, c % RING, :, 0:width], view).then_inc(raw_landed[c % RING], 16)

            def pick(v, n, col, width):
                return v[bass.ds(n, 1), :, :, bass.ds(col, width)][0]

            for l in range(DEPTH):
                for b in range(2):
                    for s in range(8):
                        load(v_mem[l * 8 + s, :, :, b * NB:(b + 1) * NB])

            def layer(L):
                for name, col, width, _k in IN_BLOCKS:
                    for s in range(8):
                        load(pick(v_in, L * 8 + s, col, width), width)

                def gate_block(n):
                    for br in BRANCHES:
                        r = BRANCH_ROW[br]
                        for s in range(8):
                            load(pick(v_in, L * 8 + s, n * NB + (G0 + r * D), NB))
                        for s in range(2):
                            load(pick(v_br, L * 8 + (2 * r + s), n * NB, NB))

                repeat(sp, 4, [(at, 40)], gate_block)
                for n in range(4):
                    for s in range(8):
                        load(pick(v_out, L * 8 + s, n * NB, NB))

            repeat(sp, DEPTH, [(at, LAYER_CHUNKS)], layer)
            for name, col, width, _k in IN2_BLOCKS:
                for s in range(8):
                    load(v_in2[s, :, :, col:col + width], width)
            for v, n in ((v_uq, 3), (v_ukv, 4)):
                for b in range(n):
                    for s in range(2):
                        load(v[s, :, :, b * NB:(b + 1) * NB])

            def gate2_block(n):
                for g, v in ((0, v_mla), (1, v_dil)):
                    for s in range(8):
                        load(v_in2[s, :, :, bass.ds(n * NB + (G2 + g * D), NB)])
                    for s in range(4):
                        load(v[s, :, :, bass.ds(n * NB, NB)])

            repeat(sp, 4, [(at, 24)], gate2_block)
            for n in range(4):
                for s in range(8):
                    load(v_o2[s, :, :, n * NB:(n + 1) * NB])

            def gt(j):
                for s in range(8):
                    load(v_gu[s, :, :, bass.ds(j * NB, NB)])

            def up(j):
                for s in range(8):
                    load(v_gu[s, :, :, bass.ds(j * NB + N_FF * NB, NB)])

            def down(j):
                for n in range(4):
                    for s in range(2):
                        load(pick(v_down, j * 2 + s, n * NB, NB))

            for s in range(8):
                load(v_gu[s, :, :, 0:NB])
            for s in range(8):
                load(v_gu[s, :, :, N_FF * NB:(N_FF + 1) * NB])

            def ffn(i):
                gt(i + 1)
                down(i)
                up(i + 1)

            repeat(sp, N_FF - 1, [(at, 24)], ffn)
            for n in range(4):
                for s in range(2):
                    load(v_down[2 * (N_FF - 1) + s, :, :, n * NB:(n + 1) * NB])

        @block.tensor
        def _(pe):
            ch, bl = Tally(RING), Tally(2)
            pt, ps, po = Tally(2), Tally(1), Tally(1)
            smx, nrm, yr, cpair, lvl, xno = Tally(), Tally(), Tally(), Tally(), Tally(), Tally()
            idx, rop, dec, gu = Tally(), Tally(), Tally(), Tally()

            def multiply(ah, al, kk, kt, width=NB, phase=None):
                b = bl.take()
                if b >= 2:
                    pe.wait_ge(gm_free[b % 2], bl.round_value(b))
                for s in range(kt // CK):
                    c = ch.take()
                    pe.wait_ge(lo_done, ch.value(c + 1))
                    for j in range(CK):
                        k = s * CK + j
                        for t in range(TT):
                            tok = slice(t * P, (t + 1) * P)
                            for q, (a, w) in enumerate(((ah, w_hi), (ah, w_lo), (al, w_hi))):
                                mm = nc.tensor.matmul(G[b % 2][:, t, 0:width], a[:, kk + k, tok], w[:, c % RING, j, 0:width],
                                                      start=(k == 0 and q == 0), stop=(k == kt - 1 and q == 2))
                    mm.then_inc(mm_done, 1)
                    if phase:
                        phase()

            def turn(pieces):
                i = pt.take()
                if i >= 2:
                    (hold if pieces[0][0].shape[-1] < P else plain)(pe, pt_free[i % 2], pt.round_value(i))
                for src, col in pieces:
                    n = src.shape[-1]
                    mm = nc.tensor.transpose(PT[i % 2][0:n, col:col + P], src, ident[:])
                mm.then_inc(pt_full, 1)
                return i

            def evacuated(name, table, tally=bl):
                b = table[name]
                pe.wait_ge(gm_free[b % 2], tally.round_value(b) + 1)

            def feed(src, kt):
                for k in range(0, kt, 2):
                    i = turn([(src[:, t, (k + j) * P:(k + j + 1) * P], (2 * j + t) * P) for j in range(2) for t in range(TT)])
                turns_read(pe, pt, i)

            def tail():
                r = yr.take()
                pe.wait_ge(y_ready, yr.value(r + 2))
                turn([(yz[:, r % 2, t, :], t * P) for t in range(TT)])

            def soft(q, k, v, extra=None):
                i = turn([(q(t), t * P) for t in range(TT)] + [(k(t), (2 + t) * P) for t in range(TT)])
                if extra:
                    i = turn([(extra(t), t * P) for t in range(TT)])
                yield
                s = ps.take()
                turns_read(pe, pt, i, both=bool(extra))
                pe.wait_ge(ps_free, ps.value(s + 1))
                for t in range(TT):
                    mm = nc.tensor.matmul(PS[:, t * T:(t + 1) * T], qk_t[:, t * P:(t + 1) * P], qk_t[:, T:2 * T], start=True, stop=not extra)
                    if extra:
                        mm = nc.tensor.matmul(PS[:, t * T:(t + 1) * T], qr_t[:, t * P:(t + 1) * P], kr_t, start=False, stop=True)
                mm.then_inc(ps_full, 1)
                yield
                e = smx.take()
                pe.wait_ge(exp_done, smx.value(e + 1))
                i = turn([(pr[:, t, a * P:(a + 1) * P], (2 * a + t) * P) for a in range(TT) for t in range(TT)])
                yield
                o = po.take()
                turns_read(pe, pt, i, both=False)
                pe.wait_ge(y_ready, po.value(o + 1))
                for t in range(TT):
                    for a in range(TT):
                        mm = nc.tensor.matmul(PO[:, t * P:(t + 1) * P], p_t[:, a, t * P:(t + 1) * P], v(a), start=(a == 0), stop=(a == TT - 1))
                mm.then_inc(po_full, 1)
                yield
                tail()
                yield

            def hd(z, h, w=P):
                return lambda t: z[:, t, h * w:h * w + P]

            def branch_c():
                for name in ("c_q", "c_z"):
                    evacuated(name, LAYER_BLOCK)
                for g in range(2):
                    for name in ("c_f", "c_q"):
                        turn([(u[name][:, t, (2 * g + i) * P:(2 * g + i + 1) * P], (2 * i + t) * P) for i in range(2) for t in range(TT)])
                        yield
                    last_turn = pt.k
                    for l in range(LEVELS + 1):
                        s = ps.take()
                        if l == 0:
                            turns_read(pe, pt, last_turn - 1, both=False)
                            pe.wait_ge(ks_ready, lvl.value(lvl.k + 1))
                        else:
                            n = lvl.take()
                            pe.wait_ge(qp_ready, lvl.value(n + 1))
                            pe.wait_ge(ks_ready, lvl.value(n + 1))
                        pe.wait_ge(ps_free, ps.value(s + 1))
                        kb, qb = ks_buf(l), qp_buf(l)
                        for i in range(2):
                            if l < LEVELS:
                                for a in (2 * i * P, (2 * i + 1) * P):
                                    mm = nc.tensor.matmul(PS[:, a:a + P], kb[:, a:a + P], qb[:, a:a + P], start=True, stop=True)
                            else:
                                a = 2 * i * P
                                mm = nc.tensor.matmul(PS[:, i * P:(i + 1) * P], kb[:, a:a + P], qb[:, a + P:a + 2 * P], start=True, stop=True)
                        mm.then_inc(ps_full, 1)
                        yield
                    n = cpair.take()
                    pe.wait_ge(acc_ready, cpair.value(n + 1))
                    for i in range(2):
                        v = hd(u["c_i"], 2 * g + i)
                        o = po.take()
                        pe.wait_ge(y_ready, po.value(o + 1))
                        a = 2 * i * P
                        nc.tensor.matmul(PO[:, 0:P], acc[:, a:a + P], v(0), start=True, stop=True)
                        nc.tensor.matmul(PO[:, P:2 * P], acc_off[:, i * P:(i + 1) * P], v(0), start=True, stop=False)
                        nc.tensor.matmul(PO[:, P:2 * P], acc[:, a + P:a + 2 * P], v(1), start=False, stop=True).then_inc(po_full, 1)
                        yield
                        tail()
                        yield

            def branch_a():
                for name in ("a_qi", "a_kw"):
                    evacuated(name, LAYER_BLOCK)
                yield
                yield
                n = idx.take()
                hold(pe, idx_ready, idx.value(n + 1))
                for t in range(TT):
                    turn([(u["a_kw"][:, t, 0:IDX_DIM], 0)])
                yield
                for h in range(0, IDX_HEADS, 2):
                    i = turn([(u["a_qi"][:, t, (h + j) * IDX_DIM:(h + j + 1) * IDX_DIM], (2 * j + t) * P) for j in range(2) for t in range(TT)])
                    yield
                for t in range(TT):
                    for h in range(0, IDX_HEADS, 2):
                        s = ps.take()
                        turns_read(pe, pt, i)
                        pe.wait_ge(ps_free, ps.value(s + 1))
                        for j in range(2):
                            mm = nc.tensor.matmul(PS[:, j * T:(j + 1) * T], qi_t[:, h + j, t * P:(t + 1) * P], ki_t, start=True, stop=True)
                        mm.then_inc(ps_full, 1)
                        yield
                for _ in range(8):
                    yield
                nrm.k += 2
                pe.wait_ge(heads_normed, nrm.value(nrm.k))
                for h in range(H):
                    yield from soft(hd(u["a_q"], h), hd(u["a_k"], h), hd(u["a_v"], h))

            def branch_m():
                evacuated("m_z", LAYER_BLOCK)
                yield
                yield
                nrm.k += 2
                pe.wait_ge(heads_normed, nrm.value(nrm.k))
                for h in range(H):
                    yield from soft(hd(u["m_q"], h), hd(mk, h), hd(mv, h))

            def branch_b():
                evacuated("b_v", LAYER_BLOCK)
                evacuated("b_z", LAYER_BLOCK)
                n = rop.take()
                pe.wait_ge(roped, rop.value(n + 1))
                for h in range(H):
                    i = turn([(hd(u[z], h)(t), (2 * y + t) * P) for y, z in enumerate(("b_q", "b_k")) for t in range(TT)])
                    yield
                    s = ps.take()
                    turns_read(pe, pt, i, both=False)
                    pe.wait_ge(ps_free, ps.value(s + 1))
                    for a in range(TT):
                        mm = nc.tensor.matmul(PS[:, a * T:(a + 1) * T], qk_t[:, T + a * P:T + (a + 1) * P], qk_t[:, 0:T], start=True, stop=True)
                    mm.then_inc(ps_full, 1)
                    yield
                    e = dec.take()
                    pe.wait_ge(decayed, dec.value(e + 1))
                    o = po.take()
                    pe.wait_ge(y_ready, po.value(o + 1))
                    for t in range(TT):
                        for a in range(TT):
                            mm = nc.tensor.matmul(PO[:, t * P:(t + 1) * P], p_t[:, a, t * P:(t + 1) * P], hd(u["b_v"], h)(a), start=(a == 0), stop=(a == TT - 1))
                    mm.then_inc(po_full, 1)
                    yield
                    tail()
                    yield

            def attention():
                yield from branch_c()
                yield from branch_a()
                yield from branch_m()
                yield from branch_b()

            pe.wait_ge(consts_in, CONSTS_IN)
            pe.wait_ge(mem_in, 16)
            feed(xs, KD)
            for _ in range(PRO_BLOCKS):
                multiply(xh, xl, 0, KD)

            def layer(L):
                n = xno.take()
                pe.wait_ge(xn_done, xno.value(n + 1))
                feed(xn, KD)
                side = attention()
                y = [RING]

                def phase():
                    y[0] += 1
                    for _ in range(phases_after(y[0])):
                        next(side, None)

                for name, col, width, _k in IN_BLOCKS:
                    multiply(xh, xl, 0, KD, width, phase)
                for _ in side:
                    pass
                turns_read(pe, pt, pt.k - 1, wait=hold)

                def gate_block(n):
                    for i, br in enumerate(BRANCHES):
                        multiply(xh, xl, 0, KD)
                        multiply(yh, yl, 4 * i, 4)

                repeat(pe, 4, [(ch, 40), (bl, 8)], gate_block)
                gu.k += 16
                pe.wait_ge(sig_used, gu.value(gu.k + 1))
                feed(merged, KD)
                for n in range(4):
                    multiply(xh, xl, 0, KD)

            steps = [(ch, LAYER_CHUNKS), (bl, LAYER_BLOCKS), (pt, PT_LAYER), (ps, PS_LAYER), (po, 16), (smx, 8), (nrm, 4), (yr, 16),
                     (cpair, 2), (lvl, 2 * LEVELS), (xno, 1), (idx, 1), (rop, 1), (dec, 4), (gu, 16)]
            repeat(pe, DEPTH, steps, layer, "pe layer")

            n = xno.take()
            pe.wait_ge(xn_done, xno.value(n + 1))
            feed(xn, KD)
            for name, col, width, _k in IN2_BLOCKS[:3]:
                multiply(xh, xl, 0, KD, width)
            n = xno.take()

            for name, col, width, _k in IN2_BLOCKS[3:]:
                multiply(xh, xl, 0, KD, width)
            pe.wait_ge(xn_done, xno.value(n + 1))
            for src in (cqn, ckvn):
                for k in range(0, 4, 2):
                    i = turn([(src[:, t, (k + j) * P:(k + j + 1) * P], (2 * j + t) * P) for j in range(2) for t in range(TT)])
            turns_read(pe, pt, i)
            for _ in range(3):
                multiply(yh, yl, 0, 4)
            for _ in range(4):
                multiply(yh, yl, 4, 4)

            evacuated("vd0", LAST_BLOCK)
            evacuated("vd1", LAST_BLOCK)
            nrm.k += 4
            pe.wait_ge(heads_normed, nrm.value(nrm.k))
            for h in range(HEADS2):
                for _ in soft(hd(qd, h), hd(kd, h), hd(vd, h)):
                    pass
            evacuated("ukv3", LAST_BLOCK)
            evacuated("ukv2", LAST_BLOCK)
            pe.wait_ge(rope2_ready, 1)
            turn([(krn[:, t, :], t * P) for t in range(TT)])
            for h in range(HEADS2):
                for _ in soft(hd(q2, h, QW), hd(kv2, h, 256), lambda a, h=h: kv2[:, a, h * 256 + P:(h + 1) * 256],
                              extra=lambda t, h=h: q2[:, t, h * QW + NOPE:(h + 1) * QW]):
                    pass
            turns_read(pe, pt, pt.k - 1)

            def gate2_block(n):
                for kk in (8, 0):
                    multiply(xh, xl, 0, KD)
                    multiply(yh, yl, kk, 8)

            repeat(pe, 4, [(ch, 24), (bl, 4)], gate2_block)
            gu.k += 8
            pe.wait_ge(sig_used, gu.value(gu.k + 1))
            feed(merged, KD)
            for n in range(4):
                multiply(xh, xl, 0, KD)
            n = xno.take()
            pe.wait_ge(xn_done, xno.value(n + 1))
            feed(xn, KD)
            multiply(xh, xl, 0, KD)
            multiply(xh, xl, 0, KD)
            fr = Tally(1)

            def hidden_turns():
                n = fr.take()
                pe.wait_ge(ffn_ready, fr.value(n + 1))
                for k in range(0, 4, 2):
                    turn([(hidden[:, t, (k + j) * P:(k + j + 1) * P], (2 * j + t) * P) for j in range(2) for t in range(TT)])

            def after(n, what):
                left = [n]

                def phase():
                    left[0] -= 1
                    if left[0] == 0:
                        what()
                return phase

            def ffn(i):
                multiply(xh, xl, 0, KD, phase=after(6, hidden_turns))
                turns_read(pe, pt, pt.k - 1)
                for n in range(4):
                    multiply(yh, yl, 0, 4)
                multiply(xh, xl, 0, KD)

            repeat(pe, N_FF - 1, [(ch, 24), (bl, 6), (pt, 2), (fr, 1)], ffn)
            hidden_turns()
            turns_read(pe, pt, pt.k - 1)
            for n in range(4):
                multiply(yh, yl, 0, 4)

        @block.scalar
        def _(act):
            ch, bl = Tally(RING), Tally(2)
            pt, ps, po = Tally(2), Tally(1), Tally(1)
            gu, smx, xsq, ru = Tally(), Tally(), Tally(), Tally()

            def split(width=NB):
                c = ch.take()
                act.wait_ge(raw_landed[c % RING], ch.round_value(c, 16) + 16)
                if c >= RING:
                    act.wait_ge(mm_done, ch.value(c - RING + 1))
                nc.scalar.activation(w_hi[:, c % RING, :, 0:width], raw[:, c % RING, :, 0:width], ACT.Copy).then_inc(hi_done, 1)

            def read_out(b, c_end, kind, dst, width=NB):
                if kind not in ("copy", "silu", "gate", "sigmoid"):
                    return
                act.wait_ge(mm_done, ch.value(c_end))
                g = G[b % 2][:, :, 0:width]
                if kind == "copy":
                    nc.scalar.activation(dst, g, ACT.Copy).then_inc(gm_free[b % 2], 1)
                    return
                if kind != "silu":
                    act.wait_ge(sig_used, gu.value(gu.take() + 1))
                nc.scalar.activation(dst, g, ACT.Sigmoid).then_inc(gm_free[b % 2] if kind == "sigmoid" else sig_done, 1)

            def blocks(items, prev, phase=None):
                for kind, dst, kt, width in items:
                    b, n = bl.take(), kt // CK
                    for s in range(n):
                        split(width)
                        if s == min(3, n - 1) and prev:
                            read_out(*prev)
                        if phase:
                            phase()
                    prev = (b, ch.k, kind, dst, width)
                return prev

            def evac_gain(pieces, count=True):
                i = pt.take()
                act.wait_ge(pt_full, pt.value(i + 1))
                for n, (dst, a, b, gain, r) in enumerate(pieces):
                    last = nc.scalar.activation(dst, PT[i % 2][0:r, a:b], ACT.Copy, scale=1.0 if gain is None else gain)
                last.then_inc(pt_free[i % 2], 1)

            def evac_high(dsts):
                i = pt.take()
                act.wait_ge(pt_full, pt.value(i + 1))
                for dst, a, b, gain in dsts:
                    last = nc.scalar.activation(dst, PT[i % 2][:, a:b], ACT.Copy, scale=1.0 if gain is None else gain)
                last.then_inc(pt_hi, 1)

            def feed(kt, h, kk, gain=None):
                for k in range(0, kt, 2):
                    if gain is None:
                        evac_high([(h[:, kk + k:kk + k + 2, :], 0, 512, None)])
                    else:
                        evac_high([(h[:, kk + k + j, :], j * T, (j + 1) * T, gain(k + j)) for j in range(2)])

            def tail(kk, gain):
                evac_high([(yh[:, kk, :], 0, T, gain)])

            def soft(kk, scale, gq, gk, src, extra=False):
                evac_gain([(qk_t[:, 0:T], 0, T, gq, P), (qk_t[:, T:2 * T], T, 2 * T, gk, P)])
                if extra:
                    evac_gain([(qr_t, 0, T, None, ROPE2)])
                yield
                e, s = smx.take(), ps.take()
                act.wait_ge(max_done, smx.value(e + 1))
                for t in range(TT):
                    z = PS[:, t * T:(t + 1) * T] if src is None else src[:, t, :]
                    last = nc.scalar.activation(pr[:, t, :], z, ACT.Exp, bias=nmx[:, t:t + 1], scale=scale, accum_out=esum[:, t:t + 1])
                last.then_inc(exp_done, 1)
                yield
                i = pt.take()
                act.wait_ge(pt_full, pt.value(i + 1))
                yield
                po.take()
                yield
                tail(kk, None)
                yield

            def squares_of_output():
                o = po.take()
                act.wait_ge(po_full, po.value(o + 1))
                for t in range(TT):
                    last = nc.scalar.activation(core[:, 512 + t * P:512 + (t + 1) * P], PO[:, t * P:(t + 1) * P], ACT.Square, accum_out=o_ssq[:, t:t + 1])
                last.then_inc(o_squared, 1)

            def branch_c(L):
                for g in range(2):
                    i = pt.take()
                    act.wait_ge(pt_full, pt.value(i + 1))
                    nc.scalar.activation(f2, PT[i % 2][:], ACT.Sigmoid).then_inc(pt_free[i % 2], 1)
                    yield
                    evac_gain([(q_c, 0, 512, None, P)])
                    yield
                    for l in range(LEVELS + 1):
                        ps.take()
                        yield
                    for i in range(2):
                        squares_of_output()
                        yield
                        tail(2 * g + i, hg_gain[:, 2 * g + i:2 * g + i + 1])
                        yield

            def branch_a(L):
                yield
                yield
                for t in range(TT):
                    evac_gain([(ki_t[:, t * P:(t + 1) * P], 0, P, None, IDX_DIM)])
                yield
                for h in range(0, IDX_HEADS, 2):
                    evac_gain([(qi_t[:, h:h + 2, :], 0, 512, None, IDX_DIM)])
                    yield
                for n in range(4 * TT):
                    s, r = ps.take(), ru.take()
                    act.wait_ge(ps_full, ps.value(s + 1))
                    act.wait_ge(rel_used, ru.value(r + 1))
                    nc.scalar.activation(rel[n % 2], PS[:], ACT.Relu).then_inc(ps_free, 1)
                    yield
                for _ in range(8):
                    yield
                for h in range(H):
                    yield from soft(4 + h, HD ** -0.5, qk_gain[:, 0:1], qk_gain[:, 1:2], sc)

            def branch_m(L):
                yield
                yield
                for h in range(H):
                    yield from soft(8 + h, HD ** -0.5, qk_gain[:, 2:3], qk_gain[:, 3:4], None)

            def branch_b(L):
                for h in range(H):
                    evac_gain([(qk_t[:, 0:T], 0, T, None, P), (qk_t[:, T:2 * T], T, 2 * T, None, P)])
                    yield
                    ps.take()
                    yield
                    squares_of_output()
                    yield
                    tail(12 + h, ret_gain[:, h:h + 1])
                    yield

            def squares_of_x():
                n = xsq.take()
                act.wait_ge(x_ready, xsq.value(n + 1))
                for t in range(TT):
                    last = nc.scalar.activation(xn[:, t, :], xs[:, t, :], ACT.Square, accum_out=x_ssq[:, t:t + 1])
                last.then_inc(x_sq_done, 1)

            for a, b in ((ident[:], k_ident), (ret_tab[:], k_ret), (tmp[:, 0:LEVELS * P], k_levels),
                         (seen[:].rearrange("p t s -> p (t s)"), k_seen),
                         (cos[:].rearrange("p t n -> p (t n)"), k_cos), (sin[:].rearrange("p t n -> p (t n)"), k_sin),
                         (k2[:, 0].rearrange("p t n -> p (t n)"), k_cos2), (k2[:, 1].rearrange("p t n -> p (t n)"), k_sin2)):
                act.dma_start(a, b).then_inc(consts_in, 16)
            columns = []
            for l in range(DEPTH):
                columns += [(par_l[:, l, 0:16], norm_g[l].rearrange("(k p) -> p k", p=P)), (par_l[:, l, 16:20], qk_g[l].rearrange("j p -> p j")),
                            (par_l[:, l, 20:24], ret_g[l].rearrange("h p -> p h")), (par_l[:, l, 24:28], hgrn_g[l].rearrange("h p -> p h")),
                            (lg[:, l, :], lb_logits[l].rearrange("h p -> p h"))]
            columns += [(p_mix, g_mix[0].rearrange("(k p) -> p k", p=P)), (p_ffn, g_ffn[0].rearrange("(k p) -> p k", p=P)),
                        (p_cq, g_cq[0].rearrange("(k p) -> p k", p=P)), (p_ckv, g_ckv[0].rearrange("(k p) -> p k", p=P))]
            columns += [(p_h2[:, i:i + 1], g.rearrange("l p -> p l")) for i, g in enumerate((g_qn, g_kn, g_qd, g_kd))]
            columns += [(g2[:, i, :], g.partition_broadcast(P).rearrange("p l n -> p (l n)")) for i, g in enumerate((g_qr, g_kr))]
            assert len(columns) == N_PARS
            with nc.allow_non_contiguous_dma(reason="parameters as columns, a few kilobytes"):
                for a, b in columns:
                    act.dma_start(a, b).then_inc(pars_in, 16)
            act.wait_ge(lb_shifted, 1)
            nc.scalar.activation(le[:], lg[:], ACT.Exp).then_inc(lb_exp, 1)
            feed(KD, xh, 0)
            prev = blocks([("copy", area(Q0 + 1024 * i, 0, NB), KD, NB) for i in range(PRO_BLOCKS)], None)
            read_out(*prev)
            act.wait_ge(mkv_out, 16)

            def layer(L):
                squares_of_x()
                act.wait_ge(pars_now, xsq.value(xsq.k))
                feed(KD, xh, 0, lambda k: x_gain[:, k:k + 1])
                act.wait_ge(x_out, xsq.round_value(xsq.k - 1, 16) + 16)

                def attention():
                    yield from branch_c(L)
                    yield from branch_a(L)
                    yield from branch_m(L)
                    yield from branch_b(L)

                side = attention()
                y = [0]

                def phase():
                    y[0] += 1
                    for _ in range(phases_after(y[0])):
                        next(side)

                prev = blocks([(k, u[name], KD, width) for name, col, width, k in IN_BLOCKS], None, phase)
                read_out(*prev)
                for _ in side:
                    pass

                def gate_block(n):
                    prev = blocks([("sigmoid", sig, KD, NB), ("merge", None, 4, NB)] * 4, None)

                repeat(act, 4, [(ch, 40), (bl, 8), (gu, 4)], gate_block)
                feed(KD, xh, 0)
                blocks([("add", None, KD, NB)] * 4, None)

            repeat(act, DEPTH, [(ch, LAYER_CHUNKS), (bl, LAYER_BLOCKS), (pt, PT_LAYER), (ps, PS_LAYER), (po, 16), (gu, 16), (smx, 8),
                                (xsq, 1), (ru, 8)], layer, "act layer")

            squares_of_x()
            feed(KD, xh, 0, lambda k: p_mix[:, k:k + 1])
            act.wait_ge(x_out, 16 * (DEPTH + 1))
            prev = blocks([(k, u[name], KD, width) for name, col, width, k in IN2_BLOCKS[:4]], None)
            for i, src in enumerate((cqn, ckvn)):
                b = LAST_BLOCK[("cq", "ckv")[i]]
                act.wait_ge(gm_free[b % 2], b // 2 + 1)
                for t in range(TT):
                    last = nc.scalar.activation(core[:, (2 * i + t) * NB:(2 * i + t + 1) * NB], src[:, t, :], ACT.Square, accum_out=x_ssq[:, 2 * i + t:2 * i + t + 1])
            last.then_inc(x_sq_done, 1)
            prev = blocks([(k, u[name], KD, width) for name, col, width, k in IN2_BLOCKS[4:]], prev)
            feed(4, yh, 0, lambda k: p_cq[:, k:k + 1])
            feed(4, yh, 4, lambda k: p_ckv[:, k:k + 1])
            prev = blocks([(k, u[name], 4, width) for name, col, width, k in UQ_BLOCKS + UKV_BLOCKS], prev)
            read_out(*prev)
            for h in range(HEADS2):
                for _ in soft(h, 1.0, p_h2[:, 2:3], p_h2[:, 3:4], sc):
                    pass
            evac_gain([(kr_t, 0, T, None, ROPE2)])
            for h in range(HEADS2):
                for _ in soft(8 + h, QW ** -0.5, p_h2[:, 0:1], p_h2[:, 1:2], None, extra=True):
                    pass

            def gate2_block(n):
                for g in range(2):
                    b = bl.take()
                    for s in range(8):
                        split()
                    for s in range(4):
                        split()
                    bl.take()
                    act.wait_ge(gm_free[b % 2], bl.round_value(b) + 1)
                    nc.scalar.activation(sig, sig, ACT.Sigmoid).then_inc(sig_done, 1)

            repeat(act, 4, [(ch, 24), (bl, 4)], gate2_block)
            gu.k += 8
            feed(KD, xh, 0)
            blocks([("add", None, KD, NB)] * 4, None)
            squares_of_x()
            feed(KD, xh, 0, lambda k: p_ffn[:, k:k + 1])
            blocks([("gate", sig, KD, NB), ("up", None, KD, NB)], None)

            def ffn(i):
                gate = (bl.take(), ch.k + 8, "gate", sig, NB)
                for s in range(8):
                    split()
                for n in range(4):
                    bl.take()
                    for s in range(2):
                        split()
                        if (n, s) == (0, 0):
                            feed(4, yh, 0)
                        if (n, s) == (1, 1):
                            read_out(*gate)
                bl.take()
                for s in range(8):
                    split()

            repeat(act, N_FF - 1, [(ch, 24), (bl, 6), (pt, 2), (gu, 1)], ffn)
            feed(4, yh, 0)
            for n in range(4):
                for s in range(2):
                    split()

        @block.vector
        def _(dve):
            ch, bl = Tally(RING), Tally(2)
            pt, ps, po = Tally(2), Tally(), Tally()
            sg, smx, xr, hi, osc, yr, hs, ru, idx, chain = (Tally() for _ in range(10))
            V = nc.vector

            def link(ins):
                ins.then_inc(dve_chain, 1)
                hold(dve, dve_chain, chain.value(chain.take() + 1))

            def split(width=NB):
                c = ch.take()
                dve.wait_ge(hi_done, ch.value(c + 1))
                if c >= RING:
                    dve.wait_ge(mm_done, ch.value(c - RING + 1))
                V.tensor_tensor(w_lo[:, c % RING, :, 0:width], raw[:, c % RING, :, 0:width],
                                w_hi[:, c % RING, :, 0:width].bitcast(F32), ALU.subtract).then_inc(lo_done, 1)

            with_bias = False

            def read_out(b, c_end, kind, dst, width=NB):
                g = G[b % 2][:, :, 0:width]
                if kind in ("silu", "gate"):
                    dve.wait_ge(sig_done, sg.value(sg.take() + 1))
                elif kind in ("merge", "merge0", "up", "add", "bias"):
                    dve.wait_ge(mm_done, ch.value(c_end))
                if kind == "silu":
                    V.tensor_tensor(dst, g, dst, ALU.mult).then_inc(gm_free[b % 2], 1)
                elif kind == "gate":
                    V.tensor_tensor(dst, g, sig, ALU.mult).then_inc(gm_free[b % 2], 1)
                    dve.wait_ge(gm_free[b % 2], bl.round_value(b) + 1)
                    dve.sem_inc(sig_used, 1)
                elif kind == "up":
                    V.tensor_tensor(dst, g, dst, ALU.mult).then_inc(gm_free[b % 2], 1)
                    dve.wait_ge(gm_free[b % 2], bl.round_value(b) + 1)
                    dve.sem_inc(ffn_ready, 1)
                elif kind == "add":
                    V.tensor_tensor(dst, g, dst, ALU.add).then_inc(gm_free[b % 2], 1)
                elif kind == "bias":
                    V.tensor_tensor(sig, g, dst, ALU.add).then_inc(gm_free[b % 2], 1)
                elif kind in ("merge", "merge0"):
                    if with_bias:
                        dve.wait_ge(sig_done, sg.value(sg.take() + 1))
                    else:
                        dve.wait_ge(gm_free[(b - 1) % 2], bl.round_value(b - 1) + 1)
                    V.tensor_tensor(sig, g, sig, ALU.mult).then_inc(gm_free[b % 2], 1)
                    dve.wait_ge(gm_free[b % 2], bl.round_value(b) + 1)
                    if kind == "merge0":
                        V.tensor_copy(dst, sig).then_inc(sig_used, 1)
                    else:
                        V.tensor_tensor(dst, sig, dst, ALU.add).then_inc(sig_used, 1)

            def blocks(items, prev, phase=None):
                for kind, dst, kt, width in items:
                    b, n = bl.take(), kt // CK
                    for s in range(n):
                        split(width)
                        if s == min(3, n - 1) and prev:
                            read_out(*prev)
                        if phase:
                            phase()
                    prev = (b, ch.k, kind, dst, width)
                return prev

            def low(pieces):
                i, n = pt.take(), hi.take()
                dve.wait_ge(pt_hi, hi.value(n + 1))
                for h, l, a, b, gain in pieces:
                    z = PT[i % 2][:, a:b]
                    if gain is None:
                        if h.ndim == 3:
                            z = z.rearrange("p (k t) -> p k t", t=T)
                        last = V.tensor_tensor(l, z, h.bitcast(F32), ALU.subtract)
                    else:
                        last = V.scalar_tensor_tensor(out=l, in0=z, scalar=gain, in1=h.bitcast(F32), op0=ALU.mult, op1=ALU.subtract)
                last.then_inc(pt_free[i % 2], 1)

            def feed(kt, h, l, kk, gain=None):
                for k in range(0, kt, 2):
                    if gain is None:
                        a = slice(kk + k, kk + k + 2)
                        low([(h[:, a, :], l[:, a, :], 0, 512, None)])
                    else:
                        low([(h[:, kk + k + j, :], l[:, kk + k + j, :], j * T, (j + 1) * T, gain(k + j)) for j in range(2)])

            def gated(z, scale_of_row):
                o, r = po.take(), yr.take()
                dve.wait_ge(po_full, po.value(o + 1))
                for t in range(TT):
                    last = V.scalar_tensor_tensor(out=yz[:, r % 2, t, :], in0=PO[:, t * P:(t + 1) * P], scalar=scale_of_row[:, t:t + 1],
                                                  in1=z(t), op0=ALU.mult, op1=ALU.mult)
                last.then_inc(y_ready, 1)

            def ungated(scale_of_row):
                o, r = po.take(), yr.take()
                dve.wait_ge(po_full, po.value(o + 1))
                for t in range(TT):
                    last = V.tensor_scalar(yz[:, r % 2, t, :], PO[:, t * P:(t + 1) * P], scale_of_row[:, t:t + 1], None, ALU.mult)
                last.then_inc(y_ready, 1)

            def normed(z):
                n = osc.take()
                dve.wait_ge(o_scaled, osc.value(n + 1))
                gated(z, o_rs)

            def tail(kk, gain):
                low([(yh[:, kk, :], yl[:, kk, :], 0, T, gain)])

            def soft(kk, scale, z, bias=None, slope=None, rotated=False):
                pt.take()
                if rotated:
                    pt.take()
                yield
                s, e = ps.take(), smx.take()
                dve.wait_ge(ps_full, ps.value(s + 1))
                flat = sc.rearrange("p t s -> p (t s)")
                src = sc
                if slope is not None:
                    link(V.scalar_tensor_tensor(out=flat, in0=PS[:], scalar=HD ** -0.5, in1=ret_tab[:, 512:1024], op0=ALU.mult, op1=ALU.add))
                    V.scalar_tensor_tensor(out=flat, in0=ret_tab[:, 0:512], scalar=slope, in1=flat, op0=ALU.mult, op1=ALU.add).then_inc(ps_free, 1)
                    dve.wait_ge(ps_free, ps.value(s + 2))
                elif bias is not None:
                    V.tensor_tensor(flat, PS[:], bias, ALU.add).then_inc(ps_free, 1)
                    dve.wait_ge(ps_free, ps.value(s + 2))
                else:
                    src = PS[:].rearrange("p (t s) -> p t s", t=TT)
                link(V.reduce_max(mx, src, AX))
                V.tensor_scalar(nmx, mx, -scale, None, ALU.mult).then_inc(max_done, 1)
                yield
                dve.wait_ge(exp_done, smx.value(e + 1))
                r = V.reciprocal(r_e, esum)
                if src is sc:
                    link(r)
                else:
                    r.then_inc(ps_free, 1)
                i = pt.take()
                dve.wait_ge(pt_full, pt.value(i + 1))
                V.tensor_copy(p_t.rearrange("p s t -> p (s t)"), PT[i % 2][:]).then_inc(pt_free[i % 2], 1)
                yield
                if z is None:
                    ungated(r_e)
                else:
                    gated(z, r_e)
                yield
                tail(kk, None)
                yield

            def sum_heads(size=1024, width=P):
                n = hs.take()
                dve.wait_ge(heads_squared, hs.value(n + 1))
                V.reduce_sum(ssq[:, 0:size // width], squares[:, 0:size].rearrange("p (h n) -> p h n", n=width), AX).then_inc(heads_summed, 1)

            def hd(z, h):
                return lambda t: z[:, t, h * P:(h + 1) * P]

            def branch_c():
                for g in range(2):
                    i = pt.take()
                    turns_read(dve, pt, i, both=False)
                    for j in range(2):
                        h = 2 * g + j
                        last = V.tensor_scalar(f2[:, j * T:(j + 1) * T], f2[:, j * T:(j + 1) * T], oml[:, h:h + 1], lb[:, h:h + 1], ALU.mult, ALU.add)
                    link(last)
                    for a, b in zip(prod[:-1], prod[1:]):
                        e = a.rearrange("p (n two) -> p n two", two=2)
                        last = V.tensor_tensor(b, e[:, :, 0], e[:, :, 1], ALU.mult)
                        if b is not prod[-1]:
                            link(last)
                    last.then_inc(gates_ready, 1)
                    yield
                    i = pt.take()
                    turns_read(dve, pt, i, both=False)
                    V.tensor_tensor(qp[0], q_c, f2, ALU.mult).then_inc(qp_ready, 1)
                    link(V.memset(acc, 0.0))
                    yield
                    for l in range(LEVELS + 1):
                        if 1 <= l < LEVELS:
                            m = HALVES[l - 1]
                            old = qp_buf(l).rearrange("p (n two m) -> p n two m", two=2, m=m)
                            new = qp_buf(l + 1).rearrange("p (n two m) -> p n two m", two=2, m=m)
                            left = prod[l - 1].rearrange("p (n two) -> p n two", two=2)[:, :, 0].unsqueeze(2).broadcast_to([P, 256 // m, m])
                            V.tensor_copy(new[:, :, 0, :], old[:, :, 0, :])
                            V.tensor_tensor(new[:, :, 1, :], old[:, :, 1, :], left, ALU.mult).then_inc(qp_ready, 1)
                        s = ps.take()
                        hold(dve, ps_full, ps.value(s + 1))
                        if l < LEVELS:
                            mask = levels[:, l, :].unsqueeze(1).broadcast_to([P, 4, P])
                            V.copy_predicated(acc.rearrange("p (a t) -> p a t", t=P), mask, PS[:].rearrange("p (a t) -> p a t", t=P)).then_inc(ps_free, 1)
                            dve.wait_ge(ps_free, ps.value(s + 2))
                        else:
                            V.tensor_copy(acc_off, PS[:, 0:2 * P]).then_inc(ps_free, 1)
                            dve.wait_ge(ps_free, ps.value(s + 2))
                            dve.sem_inc(acc_ready, 1)
                        yield
                    for j in range(2):
                        normed(hd(u["c_z"], 2 * g + j))
                        yield
                        tail(2 * g + j, hg_gain[:, 2 * g + j:2 * g + j + 1])
                        yield

            def branch_a():
                sum_heads()
                yield
                sum_heads()
                yield
                pt.take()
                pt.take()
                n = idx.take()
                dve.wait_ge(idx_ready, idx.value(n + 1))
                link(V.tensor_copy(score, seen[:]))
                yield
                for h in range(0, IDX_HEADS, 2):
                    pt.take()
                    yield
                for t in range(TT):
                    for h in range(0, IDX_HEADS, 2):
                        s = ps.take()
                        n = ru.take()
                        dve.wait_ge(ps_free, ps.value(s + 2))
                        for j in range(2):
                            ins = V.scalar_tensor_tensor(out=score[:, t, :], in0=rel[(s - PS_C) % 2][:, j * T:(j + 1) * T], scalar=wis[:, t, h + j:h + j + 1],
                                                         in1=score[:, t, :], op0=ALU.mult, op1=ALU.add)
                            if j == 0:
                                link(ins)
                        ins.then_inc(rel_used, 1)
                        hold(dve, rel_used, ru.value(n + 3))
                        yield
                for r in range(N_SEL // 8):
                    for t in range(TT):
                        top = top8[:, 8 * t:8 * t + 8]
                        link(V.max(top, score[:, t, :]))
                        link(V.match_replace(score[:, t, :], top, score[:, t, :], -3e38))
                    if r == N_SEL // 8 - 1:
                        link(V.tensor_scalar(score, score, -2e38, -BIG, ALU.is_gt, ALU.mult))
                    yield
                for h in range(H):
                    yield from soft(4 + h, HD ** -0.5, hd(u["a_z"], h), bias=score.rearrange("p t s -> p (t s)"))

            def branch_m():
                sum_heads()
                yield
                sum_heads()
                yield
                for h in range(H):
                    yield from soft(8 + h, HD ** -0.5, hd(u["m_z"], h))

            def branch_b():
                for h in range(H):
                    pt.take()
                    yield
                    s = ps.take()
                    dve.wait_ge(ps_full, ps.value(s + 1))
                    V.tensor_tensor(p_t.rearrange("p s t -> p (s t)"), PS[:], ret_tab[:, h * 512:(h + 1) * 512], ALU.mult).then_inc(ps_free, 1)
                    dve.wait_ge(ps_free, ps.value(s + 2))
                    dve.sem_inc(decayed, 1)
                    yield
                    normed(hd(u["b_z"], h))
                    yield
                    tail(12 + h, ret_gain[:, h:h + 1])
                    yield

            def normalize_x():
                n = xr.take()
                dve.wait_ge(x_rs_done, xr.value(n + 1))
                for t in range(TT):
                    last = V.tensor_scalar(xn[:, t, :], xs[:, t, :], x_rs[:, t:t + 1], None, ALU.mult)
                last.then_inc(xn_done, 1)

            dve.sem_inc(ps_free, 1)
            dve.sem_inc(y_ready, 1)
            dve.sem_inc(sig_used, 1)
            dve.sem_inc(rel_used, 2)
            dve.wait_ge(consts_in, CONSTS_IN)
            link(V.tensor_copy(levels[:].rearrange("p l q -> p (l q)"), tmp[:, 0:LEVELS * P]))
            dve.wait_ge(pars_in, PARS_IN)
            link(V.tensor_tensor(lt[:, 0, :], lg[:, 0, :], lg[:, 1, :], ALU.max))
            V.tensor_tensor(lg[:, 0, :], lg[:, 0, :], lt[:, 0, :], ALU.subtract)
            V.tensor_tensor(lg[:, 1, :], lg[:, 1, :], lt[:, 0, :], ALU.subtract).then_inc(lb_shifted, 1)
            dve.wait_ge(lb_exp, 1)
            link(V.tensor_tensor(lt[:, 0, :], le[:, 0, :], le[:, 1, :], ALU.add))
            link(V.reciprocal(lt[:, 1, :], lt[:, 0, :]))
            for l in range(DEPTH):
                link(V.tensor_tensor(le[:, l, :], le[:, l, :], lt[:, 1, :], ALU.mult))
            V.tensor_tensor(par_l[:, 0, 28:32], le[:, 0, :], le[:, 0, :], ALU.subtract)
            link(V.tensor_tensor(lt[:, 0, :], le[:, 0, :], le[:, 1, :], ALU.add))
            link(V.tensor_tensor(par_l[:, 1, 28:32], lt[:, 0, :], le[:, 0, :], ALU.subtract))
            for l in range(DEPTH):
                link(V.tensor_scalar(par_l[:, l, 32:36], par_l[:, l, 28:32], -1.0, 1.0, ALU.mult, ALU.add))
            feed(KD, xh, xl, 0)
            blocks([("copy", None, KD, NB)] * PRO_BLOCKS, None)
            dve.wait_ge(x_in, 16)
            dve.sem_inc(x_ready, 1)

            def layer(L):
                V.tensor_copy(now, par_l[:, bass.ds(L, 1), :].rearrange("p l n -> p (l n)")).then_inc(pars_now, 1)
                n = xr.k
                dve.wait_ge(pars_now, xr.value(n + 1))
                normalize_x()
                feed(KD, xh, xl, 0, lambda k: x_gain[:, k:k + 1])

                def attention():
                    yield from branch_c()
                    yield from branch_a()
                    yield from branch_m()
                    yield from branch_b()

                side = attention()
                y = [0]

                def phase():
                    y[0] += 1
                    for _ in range(phases_after(y[0])):
                        next(side)

                prev = blocks([(k, u[name], KD, width) for name, col, width, k in IN_BLOCKS], None, phase)
                read_out(*prev)
                for _ in side:
                    pass

                def gate_block(n):
                    items = []
                    for i in range(4):
                        items += [("sigmoid", None, KD, NB), ("merge" if i else "merge0", merged[:, :, bass.ds(n * NB, NB)], 4, NB)]
                    read_out(*blocks(items, None))

                repeat(dve, 4, [(ch, 40), (bl, 8)], gate_block)
                feed(KD, xh, xl, 0)
                dve.wait_ge(x_back, xr.round_value(xr.k, 16))
                prev = blocks([("add", xs[:, :, i * NB:(i + 1) * NB], KD, NB) for i in range(4)], None)
                read_out(*prev)
                dve.wait_ge(gm_free[prev[0] % 2], bl.round_value(prev[0]) + 1)
                dve.sem_inc(x_ready, 1)

            repeat(dve, DEPTH, [(ch, LAYER_CHUNKS), (bl, LAYER_BLOCKS), (pt, PT_LAYER), (hi, 16 + 16), (ps, PS_LAYER), (po, 16), (yr, 16), (sg, 4),
                                (smx, 8), (xr, 1), (osc, 8), (hs, 4), (ru, 8), (idx, 1), (chain, CHAIN["dve"])], layer, "dve layer")

            normalize_x()
            feed(KD, xh, xl, 0, lambda k: p_mix[:, k:k + 1])
            prev = blocks([(k, u[name], KD, width) for name, col, width, k in IN2_BLOCKS[:4]], None)
            n = xr.take()
            dve.wait_ge(x_rs_done, xr.value(n + 1))
            for i, src in enumerate((cqn, ckvn)):
                for t in range(TT):
                    last = V.tensor_scalar(src[:, t, :], src[:, t, :], x_rs[:, 2 * i + t:2 * i + t + 1], None, ALU.mult)
            last.then_inc(xn_done, 1)
            prev = blocks([(k, u[name], KD, width) for name, col, width, k in IN2_BLOCKS[4:]], prev)
            feed(4, yh, yl, 0, lambda k: p_cq[:, k:k + 1])
            feed(4, yh, yl, 4, lambda k: p_ckv[:, k:k + 1])
            blocks([(k, u[name], 4, width) for name, col, width, k in UQ_BLOCKS + UKV_BLOCKS], None)
            for _ in range(4):
                sum_heads()
            dve.wait_ge(dil_in, 16)
            for h in range(HEADS2):
                for _ in soft(h, 1.0, None, slope=2.0 ** -(h + 1)):
                    pass
            for size, width in ((1024, P), (1024, P), (1024, ROPE2), (1024, P), (1024, P), (TT * ROPE2, ROPE2)):
                sum_heads(size, width)
            pt.take()
            for h in range(HEADS2):
                for _ in soft(8 + h, QW ** -0.5, None, rotated=True):
                    pass
            dve.wait_ge(bias_in, 16)
            with_bias = True

            def gate2_block(n):
                items = []
                for i in range(2):
                    row = bias_rows[:, bass.ds(n * NB + i * D, NB)].unsqueeze(1).broadcast_to([P, TT, NB])
                    items += [("bias", row, KD, NB), ("merge" if i else "merge0", merged[:, :, bass.ds(n * NB, NB)], 8, NB)]
                read_out(*blocks(items, None))

            repeat(dve, 4, [(ch, 24), (bl, 4), (sg, 2)], gate2_block)
            feed(KD, xh, xl, 0)
            dve.wait_ge(x_back, 16 * (DEPTH + 1))
            prev = blocks([("add", xs[:, :, i * NB:(i + 1) * NB], KD, NB) for i in range(4)], None)
            read_out(*prev)
            dve.wait_ge(gm_free[prev[0] % 2], bl.round_value(prev[0]) + 1)
            dve.sem_inc(x_ready, 1)
            normalize_x()
            feed(KD, xh, xl, 0, lambda k: p_ffn[:, k:k + 1])
            blocks([("gate", hidden, KD, NB), ("up", hidden, KD, NB)], None)

            def ffn(i):
                up_before = (bl.k - 1, ch.k, "up", hidden, NB)
                gate = (bl.take(), ch.k + 8, "gate", hidden, NB)
                for s in range(8):
                    split()
                    if s == 3:
                        read_out(*up_before)
                downs = []
                for n in range(4):
                    b = bl.take()
                    for s in range(2):
                        split()
                        if (n, s) == (0, 0):
                            feed(4, yh, yl, 0)
                        if (n, s) == (1, 1):
                            read_out(*gate)
                        if s == 1 and n >= 2:
                            read_out(*downs[n - 2])
                    downs.append((b, ch.k, "add", xs[:, :, n * NB:(n + 1) * NB], NB))
                bl.take()
                for s in range(8):
                    split()
                    if s in (1, 3):
                        read_out(*downs[2 + s // 2])

            repeat(dve, N_FF - 1, [(ch, 24), (bl, 6), (pt, 2), (hi, 2), (sg, 1)], ffn)
            read_out(bl.k - 1, ch.k, "up", hidden, NB)
            feed(4, yh, yl, 0)
            prev = blocks([("add", xs[:, :, n * NB:(n + 1) * NB], 4, NB) for n in range(4)], None)
            read_out(*prev)
            dve.wait_ge(gm_free[prev[0] % 2], bl.round_value(prev[0]) + 1)
            dve.sem_inc(x_ready, 1)

        @block.gpsimd
        def _(pool):
            bl, xe, lyr = Tally(2), Tally(), Tally()
            pt, ps, lvl, hs, osq, pair, rel0, chain = Tally(2), Tally(), Tally(), Tally(), Tally(), Tally(), Tally(), Tally()
            V = nc.gpsimd

            def link(ins):
                ins.then_inc(pool_chain, 1)
                hold(pool, pool_chain, chain.value(chain.take() + 1))

            def evacuated(name, table):
                b = table[name]
                hold(pool, gm_free[b % 2], bl.round_value(b) + 1)

            def root(dst, src, count, n):
                link(V.tensor_scalar(src, src, 1.0 / count, EPS, ALU.mult, ALU.add))
                return V.tensor_tensor(dst, src, half[:, 0:n], ALU.pow)

            def x_norm(count=D, n=TT):
                e = xe.take()
                hold(pool, x_sq_done, xe.value(e + 1))
                root(x_rs[:, 0:n], x_ssq[:, 0:n], count, n).then_inc(x_rs_done, 1)

            def head_norm(views, heads, width=P):
                n = hs.take()
                size = TT * heads * width
                sq = squares[:, 0:size].rearrange("p (t h n) -> p t h n", t=TT, n=width)
                V.tensor_tensor(sq, views, views, ALU.mult).then_inc(heads_squared, 1)
                hold(pool, heads_summed, hs.value(n + 1))
                g = TT * heads
                link(root(rs[:, 0:g], ssq[:, 0:g], width, g))
                by = rs[:, 0:g].rearrange("p (t h) -> p t h", t=TT).unsqueeze(3).broadcast_to([P, TT, heads, width])
                ins = V.tensor_tensor(views, views, by, ALU.mult)
                return ins

            def split_heads(z, n=P):
                return z.rearrange("p t (h n) -> p t h n", n=n)

            def output_norms(n):
                for _ in range(n):
                    o = osq.take()
                    hold(pool, o_squared, osq.value(o + 1))
                    root(o_rs, o_ssq, HD, TT).then_inc(o_scaled, 1)

            def branch_c():
                for g in range(2):
                    n = pair.take()
                    hold(pool, gates_ready, pair.value(n + 1))
                    V.tensor_scalar(ks[0], f2, -1.0, 1.0, ALU.mult, ALU.add).then_inc(ks_ready, 1)
                    n = lvl.take()
                    first = ps.k
                    for l in range(1, LEVELS):
                        m = HALVES[l - 1]
                        hold(pool, ks_ready, lvl.value(lvl.k))
                        hold(pool, ps_full, ps.value(first + l))
                        old = ks_buf(l).rearrange("p (n two m) -> p n two m", two=2, m=m)
                        new = ks_buf(l + 1).rearrange("p (n two m) -> p n two m", two=2, m=m)
                        right = prod[l - 1].rearrange("p (n two) -> p n two", two=2)[:, :, 1].unsqueeze(2).broadcast_to([P, 256 // m, m])
                        V.tensor_copy(new[:, :, 1, :], old[:, :, 1, :])
                        V.tensor_tensor(new[:, :, 0, :], old[:, :, 0, :], right, ALU.mult).then_inc(ks_ready, 1)
                        lvl.take()
                    ps.k += LEVELS + 1
                    output_norms(2)

            def rotate(z, heads, n, c_s):
                a, b, d = (r[:, 0:TT * heads * n].rearrange("p (t h n) -> p t h n", t=TT, h=heads) for r in rope_t)
                x1, x2 = z[:, :, :, 0:n], z[:, :, :, n:2 * n]
                c1, s2, s1, c2 = (w.unsqueeze(2).broadcast_to([P, TT, heads, n]) for w in c_s)
                V.tensor_tensor(a, x1, c1, ALU.mult)
                V.tensor_tensor(b, x2, s2, ALU.mult)
                link(V.tensor_tensor(d, x1, s1, ALU.mult))
                link(V.tensor_tensor(x2, x2, c2, ALU.mult))
                V.tensor_tensor(x1, a, b, ALU.subtract)
                return V.tensor_tensor(x2, x2, d, ALU.add)

            pool.dma_start(xs, rows(mem[0])).then_inc(mem_in, 16)
            link(V.memset(half, -0.5))
            hold(pool, pt_full, KD // 2)
            pool.dma_start(xs, rows(x[0])).then_inc(x_in, 16)
            for q in range(2):
                hold(pool, gm_free[q], PRO_BLOCKS // 2)
            pool.dma_start(mkv_kept.rearrange("i (t p) n -> p (i t) n", p=P),
                           arena[:, Q0:Q0 + 4096].rearrange("p (i n) -> p i n", n=NB)).then_inc(mkv_out, 16)
            hold(pool, mkv_out, 16)

            def layer(L):
                n = lyr.take()
                hold(pool, x_ready, lyr.value(n + 1))
                pool.dma_start(rows(x_kept), xs).then_inc(x_out, 16)
                pool.dma_start(arena[:, M_0:M_0 + 2048].rearrange("p (i n) -> p i n", n=NB),
                               mkv_kept.rearrange("(l i) (t p) n -> l p (i t) n", l=DEPTH, p=P)[bass.ds(L, 1)][0]).then_inc(mkv_in, 16)
                x_norm()
                branch_c()
                turns_read(pool, pt, 8 + PT_C - 1, wait=hold)
                for name in ("a_q", "a_k"):
                    evacuated(name, LAYER_BLOCK)
                    head_norm(split_heads(u[name]), H).then_inc(heads_normed, 1)
                evacuated("a_kw", LAYER_BLOCK)
                hold(pool, heads_normed, hs.value(hs.k))
                V.tensor_scalar(wis, u["a_kw"][:, :, IDX_DIM:], IDX_HEADS ** -0.5 * IDX_DIM ** -0.5, None, ALU.mult).then_inc(idx_ready, 1)
                hold(pool, ps_full, ps0.value(PS_SEL))
                hold(pool, mkv_in, lyr.round_value(n, 16) + 16)
                evacuated("m_q", LAYER_BLOCK)
                head_norm(split_heads(u["m_q"]), H).then_inc(heads_normed, 1)
                head_norm(split_heads(mk), H).then_inc(heads_normed, 1)
                evacuated("b_q", LAYER_BLOCK)
                evacuated("b_k", LAYER_BLOCK)
                for i, name in enumerate(("b_q", "b_k")):
                    ins = rotate(split_heads(u[name]), H, 64, (cos[:], sin[:], sin[:], cos[:]))
                    if i:
                        ins.then_inc(roped, 1)
                    else:
                        link(ins)
                output_norms(4)
                turns_read(pool, pt, 8 + PT_ATT - 1, wait=hold)
                hold(pool, x_out, lyr.round_value(n, 16) + 16)
                pool.dma_start(xs, rows(x_kept)).then_inc(x_back, 16)
                pt.k += PT_LAYER
                ps0.k += PS_LAYER
                ps.k += PS_LAYER - PS_C
                bl.k += LAYER_BLOCKS

            ps0 = Tally()
            repeat(pool, DEPTH, [(bl, LAYER_BLOCKS), (pt, PT_LAYER), (ps, PS_LAYER), (ps0, PS_LAYER), (lyr, 1), (xe, 1), (pair, 2), (lvl, 2 * LEVELS),
                                 (hs, 4), (osq, 8), (chain, CHAIN["pool"])], layer, "pool layer")

            hold(pool, x_ready, DEPTH + 1)
            pool.dma_start(rows(x_kept), xs).then_inc(x_out, 16)
            pool.dma_start(ret_tab[:, 0:1024], k_dil).then_inc(dil_in, 16)
            x_norm()
            x_norm(NB, 4)
            bl.k = 0
            for name, z in (("qd1", qd), ("kd1", kd)):
                evacuated(name[:-1] + "0", LAST_BLOCK)
                evacuated(name, LAST_BLOCK)
                for i in range(2):
                    head_norm(split_heads(z[:, :, i * NB:(i + 1) * NB]), 4).then_inc(heads_normed, 1)
            hold(pool, heads_normed, hs.value(hs.k))
            for q in range(2):
                for k, (j, f) in enumerate(((0, 0), (1, 1), (0, 1), (1, 0))):
                    gain = g2[:, q, 32 * j:32 * j + 32].unsqueeze(1).broadcast_to([P, TT, 32])
                    last = V.tensor_tensor(rope2_tab[:, q, k], k2[:, f], gain, ALU.mult)
            link(last)
            for i in range(3):
                evacuated(f"uq{i}", LAST_BLOCK)
            for i in range(4):
                evacuated(f"ukv{i}", LAST_BLOCK)
            q_h = q2.rearrange("p t (h n) -> p t h n", n=QW)
            k_h = kv2.rearrange("p t (h n) -> p t h n", n=2 * P)
            kr_h = krn.rearrange("p t (h n) -> p t h n", h=1)
            for i, (z, h, w) in enumerate(((q_h[:, :, 0:4, 0:NOPE], 4, P), (q_h[:, :, 4:8, 0:NOPE], 4, P), (q_h[:, :, :, NOPE:], 8, ROPE2),
                              (k_h[:, :, 0:4, 0:P], 4, P), (k_h[:, :, 4:8, 0:P], 4, P), (kr_h, 1, ROPE2))):
                link(head_norm(z, h, w))
            tab = lambda q: tuple(rope2_tab[:, q, k] for k in range(4))
            link(rotate(q_h[:, :, :, NOPE:], HEADS2, 32, tab(0)))
            rotate(kr_h, 1, 32, tab(1)).then_inc(rope2_ready, 1)
            turns_read(pool, pt, PT_LAST - 1, wait=hold)
            pool.dma_start(bias_rows, b_gate.partition_broadcast(P).rearrange("p l n -> p (l n)")).then_inc(bias_in, 16)
            hold(pool, x_out, 16 * (DEPTH + 1))
            pool.dma_start(xs, rows(x_kept)).then_inc(x_back, 16)
            x_norm()
            hold(pool, x_ready, DEPTH + 3)
            pool.dma_start(rows(out[0]), xs).then_inc(all_out, 16)
            hold(pool, all_out, 16)


N_PARS = 5 * DEPTH + 10
PARS_IN = 16 * N_PARS
CONSTS_IN = 16 * 8

INPUTS = ['x', 'mem', 'norm_g', 'w_in', 'qk_norm_g', 'ret_norm_g', 'hgrn_norm_g', 'lb_logits', 'w_mem_kv', 'w_branch', 'w_out',
          'g_mix_2', 'w_in_2', 'b_gate_2', 'g_cq_2', 'w_uq_2', 'g_ckv_2', 'w_ukv_2', 'g_q_nope_2', 'g_q_rope_2', 'g_k_nope_2',
          'g_k_rope_2', 'g_q_dil_2', 'g_k_dil_2', 'w_o_mla_2', 'w_o_dil_2', 'w_o_2', 'g_ffn_2', 'w_gate_up_2', 'w_down_2']


def kernel(**inputs):
    import concourse.bacc as bacc
    from concourse.bass_utils import run_bass_kernel_spmd

    nc = bacc.Bacc("TRN2", target_bir_lowering=False, num_devices=1)
    arrays = {f"in_{name}": np.ascontiguousarray(inputs[name]) for name in INPUTS}
    arrays |= {f"const_{name}": a for name, a in constants().items()}
    handles = {name: nc.dram_tensor(name, a.shape, mybir.dt.from_np(a.dtype), kind="ExternalInput").ap() for name, a in arrays.items()}
    x_kept = nc.dram_tensor("x_kept", (T, D), F32).ap()
    mkv_kept = nc.dram_tensor("mkv_kept", (2 * DEPTH, T, W), F32).ap()
    out = nc.dram_tensor("out", (1, T, D), F32, kind="ExternalOutput").ap()
    hybrid_program(nc, *handles.values(), x_kept, mkv_kept, out)
    got = run_bass_kernel_spmd(nc, [arrays], core_ids=[0])
    return got.results[0]["out"]
```

```python
from contextlib import ExitStack

import numpy as np

import concourse.bass as bass
from concourse import mybir

F32 = mybir.dt.float32
F32R = mybir.dt.float32r
U8 = mybir.dt.uint8
ALU = mybir.AluOpType
ACT = mybir.ActivationFunctionType
AX = mybir.AxisListType.X

P = 128
D = 2048
T = 256
TT = T // P
W = 512
H = 4
HD = 128
DEPTH = 2
CHUNK = 64
N_SEL = T // 4
IDX_HEADS = 8
IDX_DIM = 64
EPS = 1e-6
KD = D // P
NB = 512
CK = 2
RING = 4
N_FF = 5632 // NB
BIG = 1e30

A0, B0, C0, M0, G0 = 0, 2632, 4680, 6728, 7752
IN_BLOCKS = [
    ("c_f", C0, NB, "copy"), ("c_i", C0 + 512, NB, "copy"), ("c_q", C0 + 1024, NB, "copy"), ("c_z", C0 + 1536, NB, "silu"),
    ("a_q", A0, NB, "copy"), ("a_k", A0 + 512, NB, "copy"), ("a_v", A0 + 1024, NB, "copy"), ("a_z", A0 + 1536, NB, "silu"),
    ("a_qi", A0 + 2048, NB, "copy"), ("a_kw", A0 + 2560, IDX_DIM + IDX_HEADS, "copy"),
    ("m_q", M0, NB, "copy"), ("m_z", M0 + 512, NB, "silu"),
    ("b_q", B0, NB, "copy"), ("b_k", B0 + 512, NB, "copy"), ("b_v", B0 + 1024, NB, "copy"), ("b_z", B0 + 1536, NB, "silu"),
]
BRANCHES = "camb"
BRANCH_ROW = {"a": 0, "b": 1, "c": 2, "m": 3}
IN2_BLOCKS = [
    ("qd0", 1088, NB, "copy"), ("qd1", 1600, NB, "copy"), ("kd0", 2112, NB, "copy"), ("kd1", 2624, NB, "copy"),
    ("vd0", 3136, NB, "copy"), ("vd1", 3648, NB, "copy"),
    ("cq", 0, NB, "copy"), ("ckv", 512, NB, "copy"), ("kr", 1024, 64, "copy"),
]
G2 = 4160
UQ_BLOCKS = [(f"uq{i}", i * NB, NB, "copy") for i in range(3)]
UKV_BLOCKS = [(f"ukv{i}", i * NB, NB, "copy") for i in range(4)]
HEADS2 = 8
NOPE, ROPE2 = 128, 64
QW = NOPE + ROPE2

PRO_BLOCKS = 2 * DEPTH
LAYER_BLOCKS = len(IN_BLOCKS) + 8 * 4 + 4
LAYER_CHUNKS = 8 * len(IN_BLOCKS) + 40 * 4 + 32
LAYER_BLOCK = {b[0]: PRO_BLOCKS + i for i, b in enumerate(IN_BLOCKS)}
LAST0 = PRO_BLOCKS + DEPTH * LAYER_BLOCKS
LAST_BLOCK = {b[0]: LAST0 + i for i, b in enumerate(IN2_BLOCKS + UQ_BLOCKS + UKV_BLOCKS)}

HALVES = [1 << i for i in range(7)]
LEVELS = 1 + len(HALVES)

CHAIN = {"dve": 70, "pool": 22}

C_PHASES = 2 * (2 + LEVELS + 1 + 4)
AMB_PHASES = (2 + 1 + IDX_HEADS // 2 + TT * IDX_HEADS // 2 + 8 + 5 * H) + (2 + 5 * H) + 4 * H
LAYER_PART = 36


def constants():
    t = np.arange(T)
    c = {}
    c["ident"] = np.eye(P, dtype=np.float32)
    log_g = np.log1p(-np.exp2(-5.0 - np.arange(H, dtype=np.float64)))
    vis = (t[:, None] // CHUNK) <= (t[None, :] // CHUNK)
    dist = np.abs(t[:, None] - t[None, :])
    ret = np.exp(log_g[:, None, None] * dist[None]) * vis[None] * HD ** -0.5
    c["ret"] = ret.reshape(H, TT, P, T).transpose(2, 0, 1, 3).reshape(P, H * TT * T).astype(np.float32)
    s, q = np.arange(P)[:, None], np.arange(P)[None, :]
    m = [s == q] + [((s // (2 * h)) == (q // (2 * h))) & (s % (2 * h) < h) & (q % (2 * h) >= h) for h in HALVES]
    c["levels"] = np.stack(m, 1).reshape(P, LEVELS * P).astype(np.float32)
    seen = (t[None, :] // CHUNK) <= (t[:, None] // CHUNK)
    c["seen"] = np.where(seen, 0.0, -BIG).reshape(TT, P, T).transpose(1, 0, 2).reshape(P, TT * T).astype(np.float32)

    def angles(dim):
        inv = np.float32(10000.0) ** (-np.arange(0, dim, 2, dtype=np.float32) / np.float32(dim))
        a = (t.astype(np.float32)[:, None] * inv[None, :].astype(np.float32)).astype(np.float64)
        return [f(a).reshape(TT, P, dim // 2).transpose(1, 0, 2).reshape(P, TT * dim // 2).astype(np.float32) for f in (np.cos, np.sin)]

    c["cos"], c["sin"] = angles(HD)
    c["cos2"], c["sin2"] = angles(ROPE2)
    count = sum(((dist % dil == 0) & (dist <= dil * (win // (2 * dil)))).astype(np.float64) for win, dil in ((128, 1), (512, 4), (2048, 16)))
    logc = np.where(count > 0, np.log(np.maximum(count, 1)), -BIG)
    c["dil"] = np.concatenate([x.reshape(TT, P, T).transpose(1, 0, 2).reshape(P, TT * T) for x in (-dist.astype(np.float64), logc)], 1).astype(np.float32)
    return c


class Tally:

    def __init__(self, unit=1, start=0):
        self.unit, self.k, self.rounds = unit, start, None

    def take(self):
        self.k += 1
        return self.k - 1

    def value(self, k):
        return k if self.rounds is None else self.rounds * self.unit + k

    def round_value(self, k, by=1):
        n = (k // self.unit) * by
        return n if self.rounds is None else self.rounds * by + n


def repeat(eng, n, tallies, body, name=None):
    with eng.Fori(0, n) as i:
        kept = []
        for t, step in tallies:
            assert step % t.unit == 0, (step, t.unit)
            kept.append((t, step, t.k, t.rounds))
            add = i * (step // t.unit)
            t.rounds = add if t.rounds is None else t.rounds + add
        body(i)
        for t, step, k, rounds in kept:
            assert t.k - k == step, (name, t.k - k, step)
            t.rounds = rounds
            t.k = k + n * step


def hybrid_program(nc, x, mem, norm_g, w_in, qk_g, ret_g, hgrn_g, lb_logits, w_mem_kv, w_branch, w_out,
                   g_mix, w_in2, b_gate, g_cq, w_uq, g_ckv, w_ukv, g_qn, g_qr, g_kn, g_kr, g_qd, g_kd,
                   w_o_mla, w_o_dil, w_o2, g_ffn, w_gu, w_down,
                   k_ident, k_ret, k_levels, k_seen, k_cos, k_sin, k_cos2, k_sin2, k_dil, x_kept, mkv_kept, out):
    with ExitStack() as ctx:
        def sb(name, shape, dt=F32):
            return ctx.enter_context(nc.sbuf_tensor(name, shape, dt))

        def psum(name):
            return ctx.enter_context(nc.psum_tensor(name, [P, 512], F32))

        def sem(name):
            return ctx.enter_context(nc.semaphore(name))

        raw = sb("raw", [P, RING, CK, NB])
        w_hi = sb("w_hi", [P, RING, CK, NB], F32R)
        w_lo = sb("w_lo", [P, RING, CK, NB], F32R)
        xh = sb("xh", [P, KD, T], F32R)
        xl = sb("xl", [P, KD, T], F32R)
        yh = sb("yh", [P, KD, T], F32R)
        yl = sb("yl", [P, KD, T], F32R)
        arena = sb("arena", [P, 13456])
        tmp = sb("tmp", [P, 4352])
        core = sb("core", [P, 2048])
        yz = sb("yz", [P, 2, TT, P])
        stat = sb("stat", [P, 192])
        ident = sb("ident", [P, P])
        ret_tab = sb("ret_tab", [P, H * TT * T])
        levels = sb("levels", [P, LEVELS, P], U8)
        seen = sb("seen", [P, TT, T])
        cos = sb("cos", [P, TT, 64])
        sin = sb("sin", [P, TT, 64])
        par_l = sb("par_l", [P, DEPTH, LAYER_PART])
        par = sb("par", [P, 96])
        k2 = sb("k2", [P, 2, TT, 32])
        g2 = sb("g2", [P, 2, ROPE2])

        def area(a, n, width):
            return arena[:, a:a + TT * width].rearrange("p (t n) -> p t n", t=TT)

        X, Q0, R0, M_0 = 0, 4096, 9360, 11408
        xs = area(X, 0, D)
        xn = area(Q0, 0, D)
        merged = xn
        u = {n: area(X + 1024 * i, 0, NB) for i, n in enumerate(("c_f", "c_i", "c_q", "c_z"))}
        u |= {n: area(X + 1024 * i, 0, NB) for i, n in enumerate(("b_q", "b_k", "b_v", "b_z"))}
        u |= {n: area(Q0 + 1024 * i, 0, NB) for i, n in enumerate(("a_q", "a_k", "a_v", "a_z", "a_qi"))}
        u["a_kw"] = area(Q0 + 5120, 0, IDX_DIM + IDX_HEADS)
        u |= {"m_q": area(R0, 0, NB), "m_z": area(R0 + 1024, 0, NB)}
        mk, mv = area(M_0, 0, NB), area(M_0 + 1024, 0, NB)
        qd, kd, vd = (area(2048 * i, 0, 1024) for i in range(3))
        q2, kv2 = area(6144, 0, 1536), area(9216, 0, 2048)
        cqn, ckvn = area(R0, 0, NB), area(R0 + 1024, 0, NB)
        krn = area(R0 + 4096 - 128, 0, 64)
        for i in range(2):
            u[f"qd{i}"], u[f"kd{i}"], u[f"vd{i}"] = (z[:, :, i * NB:(i + 1) * NB] for z in (qd, kd, vd))
        for i in range(3):
            u[f"uq{i}"] = q2[:, :, i * NB:(i + 1) * NB]
        for i in range(4):
            u[f"ukv{i}"] = kv2[:, :, i * NB:(i + 1) * NB]
        u |= {"cq": cqn, "ckv": ckvn, "kr": krn}
        merged2 = area(X, 0, D)
        xs2 = area(Q0, 0, D)
        bias_rows = [arena[:, R0:R0 + 2048], arena[:, 4096:6144]]
        hidden = area(R0, 0, NB)

        f2, q_c = tmp[:, 0:512], tmp[:, 512:1024]
        qp = [tmp[:, 1024 + 512 * i:1536 + 512 * i] for i in range(2)]
        ks = [tmp[:, 2048 + 512 * i:2560 + 512 * i] for i in range(2)]
        acc = tmp[:, 3072:3584]
        acc_off = tmp[:, 3584:3840]
        prod = [f2]
        at = 3840
        for i in range(7):
            n = 512 >> (i + 1)
            prod.append(tmp[:, at:at + n])
            at += n
        assert at <= 4352
        qi_t = tmp[0:IDX_DIM, 0:2048].rearrange("p (h t) -> p h t", h=IDX_HEADS)
        ki_t = tmp[0:IDX_DIM, 2048:2304]
        rel = [tmp[:, 2304 + 512 * i:2816 + 512 * i] for i in range(2)]
        score = tmp[:, 3328:3840].rearrange("p (t s) -> p t s", t=TT)
        squares = tmp[:, 0:1024]
        rope_t = [tmp[:, 512 * i:512 * i + 512] for i in range(3)]
        sig = tmp[:, 2048:3072].rearrange("p (t n) -> p t n", t=TT)
        kr_t = tmp[0:ROPE2, 3840:4096]
        qr_t = tmp[0:ROPE2, 4096:4352]
        rope2_tab = tmp[:, 3072:3584].rearrange("p (q k t n) -> p q k t n", q=2, k=4, t=TT)
        qk_t = core[:, 0:512]
        sc = core[:, 512:1024].rearrange("p (t s) -> p t s", t=TT)
        pr = core[:, 1024:1536].rearrange("p (t s) -> p t s", t=TT)
        p_t = core[:, 1536:2048].rearrange("p (s t) -> p s t", s=TT)

        ssq, rs = stat[:, 0:16], stat[:, 16:32]
        o_ssq, o_rs = stat[:, 32:34], stat[:, 34:36]
        x_ssq, x_rs = stat[:, 36:40], stat[:, 156:160]
        mx, nmx, esum, r_e = (stat[:, 40 + 2 * i:42 + 2 * i] for i in range(4))
        half = stat[:, 48:64]
        top8 = stat[:, 64:80]
        wis = stat[:, 80:96].rearrange("p (t h) -> p t h", t=TT)

        now = par[:, 0:LAYER_PART]
        x_gain, qk_gain, ret_gain, hg_gain, lb, oml = (now[:, i:j] for i, j in ((0, 16), (16, 20), (20, 24), (24, 28), (28, 32), (32, 36)))
        p_mix, p_ffn = par[:, 36:52], par[:, 52:68]
        p_cq, p_ckv = par[:, 68:72], par[:, 72:76]
        p_h2 = par[:, 76:80]
        lg = stat[:, 132:140].rearrange("p (l h) -> p l h", l=DEPTH)
        le = stat[:, 140:148].rearrange("p (l h) -> p l h", l=DEPTH)
        lt = stat[:, 148:156].rearrange("p (l h) -> p l h", l=2)

        G = [ctx.enter_context(nc.psum_tensor(f"G{i}", [P, TT, NB], F32)) for i in range(2)]
        PT = [psum(f"PT{i}") for i in range(2)]
        PS = psum("PS")
        PO = psum("PO")

        raw_landed = [sem(f"raw_landed{i}") for i in range(RING)]
        hi_done, lo_done, mm_done = sem("hi_done"), sem("lo_done"), sem("mm_done")
        gm_free = [sem(f"gm_free{i}") for i in range(2)]
        pt_full, pt_hi = sem("pt_full"), sem("pt_hi")
        pt_free = [sem(f"pt_free{i}") for i in range(2)]
        ps_full, ps_free = sem("ps_full"), sem("ps_free")
        po_full = sem("po_full")
        sig_done, sig_used = sem("sig_done"), sem("sig_used")
        x_sq_done, x_rs_done, xn_done = sem("x_sq_done"), sem("x_rs_done"), sem("xn_done")
        heads_squared, heads_summed, heads_normed = sem("heads_squared"), sem("heads_summed"), sem("heads_normed")
        max_done, exp_done = sem("max_done"), sem("exp_done")
        o_squared, o_scaled, y_ready = sem("o_squared"), sem("o_scaled"), sem("y_ready")
        gates_ready, ks_ready, qp_ready, acc_ready = sem("gates_ready"), sem("ks_ready"), sem("qp_ready"), sem("acc_ready")
        idx_ready, rel_used = sem("idx_ready"), sem("rel_used")
        roped = sem("roped")
        consts_in, pars_in, mem_in, x_in, x_out, x_back = (sem(n) for n in ("consts_in", "pars_in", "mem_in", "x_in", "x_out", "x_back"))
        x_ready, decayed = sem("x_ready"), sem("decayed")
        lb_shifted, lb_exp, pars_now = sem("lb_shifted"), sem("lb_exp"), sem("pars_now")
        mkv_out, mkv_in, dil_in, all_out = (sem(n) for n in ("mkv_out", "mkv_in", "dil_in", "all_out"))
        bias_in = [sem(f"bias_in{i}") for i in range(2)]
        rope2_ready = sem("rope2_ready")
        dve_chain, pool_chain = sem("dve_chain"), sem("pool_chain")
        ffn_ready = sem("ffn_ready")
        passed = sem("passed")

        def hold(eng, s, value):
            eng.wait_ge(s, value)
            eng.sem_inc(passed, 1)

        def nothing():
            pass

        def plain(eng, s, value):
            eng.wait_ge(s, value)

        def turns_read(eng, tally, i, both=True, wait=plain):
            for n in ((i - 1, i) if both else (i,)):
                wait(eng, pt_free[n % 2], tally.round_value(n) + 1)

        def cut(w):
            return w.rearrange("(c j p) n -> c p j n", j=CK, p=P)

        v_in = cut(w_in.rearrange("l k n -> (l k) n"))
        v_mem = cut(w_mem_kv.rearrange("l k n -> (l k) n"))
        v_br = cut(w_branch.rearrange("l b k n -> (l b k) n"))
        v_out = cut(w_out.rearrange("l k n -> (l k) n"))
        v_in2, v_uq, v_ukv = cut(w_in2[0]), cut(w_uq[0]), cut(w_ukv[0])
        v_mla, v_dil, v_o2, v_gu, v_down = cut(w_o_mla[0]), cut(w_o_dil[0]), cut(w_o2[0]), cut(w_gu[0]), cut(w_down[0])

        rows = lambda a: a.rearrange("(t p) n -> p t n", p=P)

        PT_C = 8 + (2 * 2 + 4)
        PT_ATT = PT_C + (2 + 4 + 3 * H) + 3 * H + 2 * H
        PT_LAYER = PT_ATT + 8
        PS_C = 2 * (LEVELS + 1)
        PS_SEL = PS_C + TT * IDX_HEADS // 2
        PS_LAYER = PS_SEL + 3 * H
        PT_DIL = KD // 2 + DEPTH * PT_LAYER + 8 + 4 + 3 * HEADS2
        PT_LAST = PT_DIL + 1 + 4 * HEADS2

        def phases_after(y):
            if 38 <= y < 38 + C_PHASES:
                return 1
            return 1 if 85 <= y < 85 + AMB_PHASES else 0

        LATENT_PHASES = (16, 18, 21, 22)
        DIL_PHASES = 4 + 5 * HEADS2 + len(LATENT_PHASES)
        MLA_PHASES = 6 + 1 + 5 * HEADS2

        def phases2_by(y):
            if y < 91:
                return max(0, min(DIL_PHASES, y - 52 if y < 76 else 23 + 2 * (y - 75)))
            return DIL_PHASES + (min(6, (y - 89) // 2) if y < 108 else min(MLA_PHASES, 6 + 2 * (y - 107)))

        def woven(main, others):
            k = 0
            while True:
                if k in others:
                    others[k]()
                elif next(main, main) is main:
                    return
                yield
                k += 1

        def ks_buf(l):
            return ks[max(l - 1, 0) % 2]

        def qp_buf(l):
            return qp[(l - 1) % 2] if l else q_c

        block = ctx.enter_context(nc.Block())

        @block.sync
        def _(sp):
            at = Tally(RING)

            def load(view, width=NB):
                c = at.take()
                if c >= RING:
                    hold(sp, lo_done, at.value(c - RING + 1))
                sp.dma_start(raw[:, c % RING, :, 0:width], view).then_inc(raw_landed[c % RING], 16)

            def pick(v, n, col, width):
                return v[bass.ds(n, 1), :, :, bass.ds(col, width)][0]

            for l in range(DEPTH):
                for b in range(2):
                    for s in range(8):
                        load(v_mem[l * 8 + s, :, :, b * NB:(b + 1) * NB])

            def layer(L):
                for name, col, width, _k in IN_BLOCKS:
                    for s in range(8):
                        load(pick(v_in, L * 8 + s, col, width), width)

                def gate_block(br, col):
                    r = BRANCH_ROW[br]
                    for s in range(8):
                        load(pick(v_in, L * 8 + s, col + (G0 + r * D), NB))
                    for s in range(2):
                        load(pick(v_br, L * 8 + (2 * r + s), col, NB))

                for n in range(4):
                    gate_block(BRANCHES[0], n * NB)

                def gate_pair(i):
                    for n in range(2):
                        for br in BRANCHES[1:]:
                            gate_block(br, i * 2 * NB + n * NB)

                repeat(sp, 2, [(at, 60)], gate_pair)
                for n in range(4):
                    for s in range(8):
                        load(pick(v_out, L * 8 + s, n * NB, NB))

            repeat(sp, DEPTH, [(at, LAYER_CHUNKS)], layer)
            for name, col, width, _k in IN2_BLOCKS:
                for s in range(8):
                    load(v_in2[s, :, :, col:col + width], width)
            for v, n in ((v_uq, 3), (v_ukv, 4)):
                for b in range(n):
                    for s in range(2):
                        load(v[s, :, :, b * NB:(b + 1) * NB])

            for n in range(4):
                for s in range(8):
                    load(v_in2[s, :, :, n * NB + G2 + D:(n + 1) * NB + G2 + D])
                for s in range(4):
                    load(v_dil[s, :, :, n * NB:(n + 1) * NB])

            def gate2_block(n):
                for s in range(8):
                    load(v_in2[s, :, :, bass.ds(n * NB + G2, NB)])
                for s in range(4):
                    load(v_mla[s, :, :, bass.ds(n * NB, NB)])

            repeat(sp, 4, [(at, 12)], gate2_block)
            for n in range(4):
                for s in range(8):
                    load(v_o2[s, :, :, n * NB:(n + 1) * NB])

            def gt(j):
                for s in range(8):
                    load(v_gu[s, :, :, bass.ds(j * NB, NB)])

            def up(j):
                for s in range(8):
                    load(v_gu[s, :, :, bass.ds(j * NB + N_FF * NB, NB)])

            def down(j):
                for n in range(4):
                    for s in range(2):
                        load(pick(v_down, j * 2 + s, n * NB, NB))

            for s in range(8):
                load(v_gu[s, :, :, 0:NB])
            for s in range(8):
                load(v_gu[s, :, :, N_FF * NB:(N_FF + 1) * NB])

            def ffn(i):
                gt(i + 1)
                down(i)
                up(i + 1)

            repeat(sp, N_FF - 1, [(at, 24)], ffn)
            for n in range(4):
                for s in range(2):
                    load(v_down[2 * (N_FF - 1) + s, :, :, n * NB:(n + 1) * NB])

        @block.tensor
        def _(pe):
            ch, bl = Tally(RING), Tally(2)
            pt, ps, po = Tally(2), Tally(1), Tally(1)
            smx, nrm, yr, cpair, lvl, xno = Tally(), Tally(), Tally(), Tally(), Tally(), Tally()
            idx, rop, dec, gu = Tally(), Tally(), Tally(), Tally()

            def multiply(ah, al, kk, kt, width=NB, phase=None):
                b = bl.take()
                if b >= 2:
                    pe.wait_ge(gm_free[b % 2], bl.round_value(b))
                for s in range(kt // CK):
                    c = ch.take()
                    pe.wait_ge(lo_done, ch.value(c + 1))
                    for j in range(CK):
                        k = s * CK + j
                        for t in range(TT):
                            tok = slice(t * P, (t + 1) * P)
                            for q, (a, w) in enumerate(((ah, w_hi), (ah, w_lo), (al, w_hi))):
                                mm = nc.tensor.matmul(G[b % 2][:, t, 0:width], a[:, kk + k, tok], w[:, c % RING, j, 0:width],
                                                      start=(k == 0 and q == 0), stop=(k == kt - 1 and q == 2))
                    mm.then_inc(mm_done, 1)
                    if phase:
                        phase()

            def turn(pieces):
                i = pt.take()
                if i >= 2:
                    (hold if pieces[0][0].shape[-1] < P else plain)(pe, pt_free[i % 2], pt.round_value(i))
                for src, col in pieces:
                    n = src.shape[-1]
                    mm = nc.tensor.transpose(PT[i % 2][0:n, col:col + P], src, ident[:])
                mm.then_inc(pt_full, 1)
                return i

            def evacuated(name, table, tally=bl):
                b = table[name]
                pe.wait_ge(gm_free[b % 2], tally.round_value(b) + 1)

            def feed(src, kt):
                for k in range(0, kt, 2):
                    i = turn([(src[:, t, (k + j) * P:(k + j + 1) * P], (2 * j + t) * P) for j in range(2) for t in range(TT)])
                turns_read(pe, pt, i)

            def tail():
                r = yr.take()
                pe.wait_ge(y_ready, yr.value(r + 2))
                turn([(yz[:, r % 2, t, :], t * P) for t in range(TT)])

            def soft(q, k, v, extra=None):
                i = turn([(q(t), t * P) for t in range(TT)] + [(k(t), (2 + t) * P) for t in range(TT)])
                if extra:
                    i = turn([(extra(t), t * P) for t in range(TT)])
                yield
                s = ps.take()
                turns_read(pe, pt, i, both=bool(extra))
                pe.wait_ge(ps_free, ps.value(s + 1))
                for t in range(TT):
                    mm = nc.tensor.matmul(PS[:, t * T:(t + 1) * T], qk_t[:, t * P:(t + 1) * P], qk_t[:, T:2 * T], start=True, stop=not extra)
                    if extra:
                        mm = nc.tensor.matmul(PS[:, t * T:(t + 1) * T], qr_t[:, t * P:(t + 1) * P], kr_t, start=False, stop=True)
                mm.then_inc(ps_full, 1)
                yield
                e = smx.take()
                pe.wait_ge(exp_done, smx.value(e + 1))
                i = turn([(pr[:, t, a * P:(a + 1) * P], (2 * a + t) * P) for a in range(TT) for t in range(TT)])
                yield
                o = po.take()
                turns_read(pe, pt, i, both=False)
                pe.wait_ge(y_ready, po.value(o + 1))
                for t in range(TT):
                    for a in range(TT):
                        mm = nc.tensor.matmul(PO[:, t * P:(t + 1) * P], p_t[:, a, t * P:(t + 1) * P], v(a), start=(a == 0), stop=(a == TT - 1))
                mm.then_inc(po_full, 1)
                yield
                tail()
                yield

            def hd(z, h, w=P):
                return lambda t: z[:, t, h * w:h * w + P]

            def branch_c():
                for name in ("c_q", "c_z"):
                    evacuated(name, LAYER_BLOCK)
                for g in range(2):
                    for name in ("c_f", "c_q"):
                        turn([(u[name][:, t, (2 * g + i) * P:(2 * g + i + 1) * P], (2 * i + t) * P) for i in range(2) for t in range(TT)])
                        yield
                    last_turn = pt.k
                    for l in range(LEVELS + 1):
                        s = ps.take()
                        if l == 0:
                            turns_read(pe, pt, last_turn - 1, both=False)
                            pe.wait_ge(ks_ready, lvl.value(lvl.k + 1))
                        else:
                            n = lvl.take()
                            pe.wait_ge(qp_ready, lvl.value(n + 1))
                            pe.wait_ge(ks_ready, lvl.value(n + 1))
                        pe.wait_ge(ps_free, ps.value(s + 1))
                        kb, qb = ks_buf(l), qp_buf(l)
                        for i in range(2):
                            if l < LEVELS:
                                for a in (2 * i * P, (2 * i + 1) * P):
                                    mm = nc.tensor.matmul(PS[:, a:a + P], kb[:, a:a + P], qb[:, a:a + P], start=True, stop=True)
                            else:
                                a = 2 * i * P
                                mm = nc.tensor.matmul(PS[:, i * P:(i + 1) * P], kb[:, a:a + P], qb[:, a + P:a + 2 * P], start=True, stop=True)
                        mm.then_inc(ps_full, 1)
                        yield
                    n = cpair.take()
                    pe.wait_ge(acc_ready, cpair.value(n + 1))
                    for i in range(2):
                        v = hd(u["c_i"], 2 * g + i)
                        o = po.take()
                        pe.wait_ge(y_ready, po.value(o + 1))
                        a = 2 * i * P
                        nc.tensor.matmul(PO[:, 0:P], acc[:, a:a + P], v(0), start=True, stop=True)
                        nc.tensor.matmul(PO[:, P:2 * P], acc_off[:, i * P:(i + 1) * P], v(0), start=True, stop=False)
                        nc.tensor.matmul(PO[:, P:2 * P], acc[:, a + P:a + 2 * P], v(1), start=False, stop=True).then_inc(po_full, 1)
                        yield
                        tail()
                        yield

            def branch_a():
                for name in ("a_qi", "a_kw"):
                    evacuated(name, LAYER_BLOCK)
                yield
                yield
                n = idx.take()
                hold(pe, idx_ready, idx.value(n + 1))
                for t in range(TT):
                    turn([(u["a_kw"][:, t, 0:IDX_DIM], 0)])
                yield
                for h in range(0, IDX_HEADS, 2):
                    i = turn([(u["a_qi"][:, t, (h + j) * IDX_DIM:(h + j + 1) * IDX_DIM], (2 * j + t) * P) for j in range(2) for t in range(TT)])
                    yield
                for t in range(TT):
                    for h in range(0, IDX_HEADS, 2):
                        s = ps.take()
                        turns_read(pe, pt, i)
                        pe.wait_ge(ps_free, ps.value(s + 1))
                        for j in range(2):
                            mm = nc.tensor.matmul(PS[:, j * T:(j + 1) * T], qi_t[:, h + j, t * P:(t + 1) * P], ki_t, start=True, stop=True)
                        mm.then_inc(ps_full, 1)
                        yield
                for _ in range(8):
                    yield
                nrm.k += 2
                pe.wait_ge(heads_normed, nrm.value(nrm.k))
                for h in range(H):
                    yield from soft(hd(u["a_q"], h), hd(u["a_k"], h), hd(u["a_v"], h))

            def branch_m():
                evacuated("m_z", LAYER_BLOCK)
                yield
                yield
                nrm.k += 2
                pe.wait_ge(heads_normed, nrm.value(nrm.k))
                for h in range(H):
                    yield from soft(hd(u["m_q"], h), hd(mk, h), hd(mv, h))

            def branch_b():
                evacuated("b_v", LAYER_BLOCK)
                evacuated("b_z", LAYER_BLOCK)
                n = rop.take()
                pe.wait_ge(roped, rop.value(n + 1))
                for h in range(H):
                    i = turn([(hd(u[z], h)(t), (2 * y + t) * P) for y, z in enumerate(("b_q", "b_k")) for t in range(TT)])
                    yield
                    s = ps.take()
                    turns_read(pe, pt, i, both=False)
                    pe.wait_ge(ps_free, ps.value(s + 1))
                    for a in range(TT):
                        mm = nc.tensor.matmul(PS[:, a * T:(a + 1) * T], qk_t[:, T + a * P:T + (a + 1) * P], qk_t[:, 0:T], start=True, stop=True)
                    mm.then_inc(ps_full, 1)
                    yield
                    e = dec.take()
                    pe.wait_ge(decayed, dec.value(e + 1))
                    o = po.take()
                    pe.wait_ge(y_ready, po.value(o + 1))
                    for t in range(TT):
                        for a in range(TT):
                            mm = nc.tensor.matmul(PO[:, t * P:(t + 1) * P], p_t[:, a, t * P:(t + 1) * P], hd(u["b_v"], h)(a), start=(a == 0), stop=(a == TT - 1))
                    mm.then_inc(po_full, 1)
                    yield
                    tail()
                    yield

            def attention():
                yield from branch_c()
                yield from branch_a()
                yield from branch_m()
                yield from branch_b()

            pe.wait_ge(consts_in, CONSTS_IN)
            pe.wait_ge(mem_in, 16)
            feed(xs, KD)
            for _ in range(PRO_BLOCKS):
                multiply(xh, xl, 0, KD)

            def layer(L):
                n = xno.take()
                pe.wait_ge(xn_done, xno.value(n + 1))
                feed(xn, KD)
                side = attention()
                y = [RING]

                def phase():
                    y[0] += 1
                    for _ in range(phases_after(y[0])):
                        next(side, None)

                for name, col, width, _k in IN_BLOCKS:
                    multiply(xh, xl, 0, KD, width, phase)
                for n in range(4):
                    multiply(xh, xl, 0, KD, phase=phase)
                    multiply(yh, yl, 0, 4, phase=phase)
                for _ in side:
                    pass
                turns_read(pe, pt, pt.k - 1, wait=hold)

                def gate_pair(i):
                    for n in range(2):
                        for k in range(1, 4):
                            multiply(xh, xl, 0, KD)
                            multiply(yh, yl, 4 * k, 4)

                repeat(pe, 2, [(ch, 60), (bl, 12)], gate_pair)
                gu.k += 16
                pe.wait_ge(sig_used, gu.value(gu.k + 1))
                feed(merged, KD)
                for n in range(4):
                    multiply(xh, xl, 0, KD)

            steps = [(ch, LAYER_CHUNKS), (bl, LAYER_BLOCKS), (pt, PT_LAYER), (ps, PS_LAYER), (po, 16), (smx, 8), (nrm, 4), (yr, 16),
                     (cpair, 2), (lvl, 2 * LEVELS), (xno, 1), (idx, 1), (rop, 1), (dec, 4), (gu, 16)]
            repeat(pe, DEPTH, steps, layer, "pe layer")

            n = xno.take()
            pe.wait_ge(xn_done, xno.value(n + 1))
            feed(xn, KD)
            latent = xno.take()

            def latent_turns(src):
                pe.wait_ge(xn_done, xno.value(latent + 1))
                for k in range(0, 4, 2):
                    turn([(src[:, t, (k + j) * P:(k + j + 1) * P], (2 * j + t) * P) for j in range(2) for t in range(TT)])

            def dilated():
                evacuated("vd0", LAST_BLOCK)
                evacuated("vd1", LAST_BLOCK)
                for _ in range(4):
                    yield
                nrm.k += 4
                pe.wait_ge(heads_normed, nrm.value(nrm.k))
                for h in range(HEADS2):
                    yield from soft(hd(qd, h), hd(kd, h), hd(vd, h))

            def latent_heads():
                for _ in range(6):
                    yield
                pe.wait_ge(rope2_ready, 1)
                turn([(krn[:, t, :], t * P) for t in range(TT)])
                yield
                for h in range(HEADS2):
                    yield from soft(hd(q2, h, QW), hd(kv2, h, 256), lambda a, h=h: kv2[:, a, h * 256 + P:(h + 1) * 256],
                                    extra=lambda t, h=h: q2[:, t, h * QW + NOPE:(h + 1) * QW])

            def attention2():
                yield from woven(dilated(), dict(zip(LATENT_PHASES, (nothing, nothing, lambda: latent_turns(cqn), lambda: latent_turns(ckvn)))))
                yield from latent_heads()

            side = attention2()
            y2 = [RING]

            def phase2():
                y2[0] += 1
                for _ in range(phases2_by(y2[0]) - phases2_by(y2[0] - 1)):
                    next(side)

            for name, col, width, _k in IN2_BLOCKS:
                multiply(xh, xl, 0, KD, width, phase2)
            for n in range(7):
                multiply(yh, yl, 8 if n < 3 else 12, 4, phase=phase2)
            for n in range(4):
                multiply(xh, xl, 0, KD, phase=phase2)
                multiply(yh, yl, 0, 8, phase=phase2)
            for _ in side:
                pass
            turns_read(pe, pt, pt.k - 1)

            def gate2_block(n):
                multiply(xh, xl, 0, KD)
                multiply(yh, yl, 8, 8)

            repeat(pe, 4, [(ch, 12), (bl, 2)], gate2_block)
            gu.k += 8
            pe.wait_ge(sig_used, gu.value(gu.k + 1))
            feed(merged2, KD)
            for n in range(4):
                multiply(xh, xl, 0, KD)
            n = xno.take()
            pe.wait_ge(xn_done, xno.value(n + 1))
            feed(merged2, KD)
            multiply(xh, xl, 0, KD)
            multiply(xh, xl, 0, KD)
            fr = Tally(1)

            def hidden_turns():
                n = fr.take()
                pe.wait_ge(ffn_ready, fr.value(n + 1))
                for k in range(0, 4, 2):
                    turn([(hidden[:, t, (k + j) * P:(k + j + 1) * P], (2 * j + t) * P) for j in range(2) for t in range(TT)])

            def after(n, what):
                left = [n]

                def phase():
                    left[0] -= 1
                    if left[0] == 0:
                        what()
                return phase

            def ffn(i):
                multiply(xh, xl, 0, KD, phase=after(6, hidden_turns))
                turns_read(pe, pt, pt.k - 1)
                for n in range(4):
                    multiply(yh, yl, 0, 4)
                multiply(xh, xl, 0, KD)

            repeat(pe, N_FF - 1, [(ch, 24), (bl, 6), (pt, 2), (fr, 1)], ffn)
            hidden_turns()
            turns_read(pe, pt, pt.k - 1)
            for n in range(4):
                multiply(yh, yl, 0, 4)

        @block.scalar
        def _(act):
            ch, bl = Tally(RING), Tally(2)
            pt, ps, po = Tally(2), Tally(1), Tally(1)
            gu, smx, xsq, ru = Tally(), Tally(), Tally(), Tally()

            def split(width=NB):
                c = ch.take()
                act.wait_ge(raw_landed[c % RING], ch.round_value(c, 16) + 16)
                if c >= RING:
                    act.wait_ge(mm_done, ch.value(c - RING + 1))
                nc.scalar.activation(w_hi[:, c % RING, :, 0:width], raw[:, c % RING, :, 0:width], ACT.Copy).then_inc(hi_done, 1)

            def read_out(b, c_end, kind, dst, width=NB):
                if kind == "bias":
                    act.wait_ge(gm_free[b % 2], bl.round_value(b) + 1)
                    nc.scalar.activation(sig, sig, ACT.Sigmoid).then_inc(sig_done, 1)
                if kind not in ("copy", "silu", "gate", "sigmoid"):
                    return
                act.wait_ge(mm_done, ch.value(c_end))
                g = G[b % 2][:, :, 0:width]
                if kind == "copy":
                    nc.scalar.activation(dst, g, ACT.Copy).then_inc(gm_free[b % 2], 1)
                    return
                if kind != "silu":
                    act.wait_ge(sig_used, gu.value(gu.take() + 1))
                nc.scalar.activation(dst, g, ACT.Sigmoid).then_inc(gm_free[b % 2] if kind == "sigmoid" else sig_done, 1)

            def blocks(items, left=(), phase=None):
                left = list(left)
                for kind, dst, kt, width in items:
                    b = bl.take()
                    for s in range(kt // CK):
                        split(width)
                        if left and left[0][1] + RING == ch.k:
                            read_out(*left.pop(0))
                        if phase:
                            phase()
                    left.append((b, ch.k, kind, dst, width))
                return left

            def finish(left):
                for block_left in left:
                    read_out(*block_left)
                return left[-1][0]

            def evac_gain(pieces):
                i = pt.take()
                act.wait_ge(pt_full, pt.value(i + 1))
                for dst, a, b, gain, r in pieces:
                    last = nc.scalar.activation(dst, PT[i % 2][0:r, a:b], ACT.Copy, scale=1.0 if gain is None else gain)
                last.then_inc(pt_free[i % 2], 1)

            def evac_high(dsts):
                i = pt.take()
                act.wait_ge(pt_full, pt.value(i + 1))
                for dst, a, b, gain in dsts:
                    last = nc.scalar.activation(dst, PT[i % 2][:, a:b], ACT.Copy, scale=1.0 if gain is None else gain)
                last.then_inc(pt_hi, 1)

            def feed(kt, h, kk, gain=None):
                for k in range(0, kt, 2):
                    if gain is None:
                        evac_high([(h[:, kk + k:kk + k + 2, :], 0, 512, None)])
                    else:
                        evac_high([(h[:, kk + k + j, :], j * T, (j + 1) * T, gain(k + j)) for j in range(2)])

            def tail(kk, gain):
                evac_high([(yh[:, kk, :], 0, T, gain)])

            def soft(kk, scale, gq, gk, src, extra=False):
                evac_gain([(qk_t[:, 0:T], 0, T, gq, P), (qk_t[:, T:2 * T], T, 2 * T, gk, P)])
                if extra:
                    evac_gain([(qr_t, 0, T, None, ROPE2)])
                yield
                e, s = smx.take(), ps.take()
                act.wait_ge(max_done, smx.value(e + 1))
                for t in range(TT):
                    z = PS[:, t * T:(t + 1) * T] if src is None else src[:, t, :]
                    last = nc.scalar.activation(pr[:, t, :], z, ACT.Exp, bias=nmx[:, t:t + 1], scale=scale, accum_out=esum[:, t:t + 1])
                last.then_inc(exp_done, 1)
                yield
                i = pt.take()
                act.wait_ge(pt_full, pt.value(i + 1))
                yield
                po.take()
                yield
                tail(kk, None)
                yield

            def squares_of_output():
                o = po.take()
                act.wait_ge(po_full, po.value(o + 1))
                for t in range(TT):
                    last = nc.scalar.activation(core[:, 512 + t * P:512 + (t + 1) * P], PO[:, t * P:(t + 1) * P], ACT.Square, accum_out=o_ssq[:, t:t + 1])
                last.then_inc(o_squared, 1)

            def branch_c(L):
                for g in range(2):
                    i = pt.take()
                    act.wait_ge(pt_full, pt.value(i + 1))
                    nc.scalar.activation(f2, PT[i % 2][:], ACT.Sigmoid).then_inc(pt_free[i % 2], 1)
                    yield
                    evac_gain([(q_c, 0, 512, None, P)])
                    yield
                    for l in range(LEVELS + 1):
                        ps.take()
                        yield
                    for i in range(2):
                        squares_of_output()
                        yield
                        tail(2 * g + i, hg_gain[:, 2 * g + i:2 * g + i + 1])
                        yield

            def branch_a(L):
                yield
                yield
                for t in range(TT):
                    evac_gain([(ki_t[:, t * P:(t + 1) * P], 0, P, None, IDX_DIM)])
                yield
                for h in range(0, IDX_HEADS, 2):
                    evac_gain([(qi_t[:, h:h + 2, :], 0, 512, None, IDX_DIM)])
                    yield
                for n in range(4 * TT):
                    s, r = ps.take(), ru.take()
                    act.wait_ge(ps_full, ps.value(s + 1))
                    act.wait_ge(rel_used, ru.value(r + 1))
                    nc.scalar.activation(rel[n % 2], PS[:], ACT.Relu).then_inc(ps_free, 1)
                    yield
                for _ in range(8):
                    yield
                for h in range(H):
                    yield from soft(4 + h, HD ** -0.5, qk_gain[:, 0:1], qk_gain[:, 1:2], sc)

            def branch_m(L):
                yield
                yield
                for h in range(H):
                    yield from soft(8 + h, HD ** -0.5, qk_gain[:, 2:3], qk_gain[:, 3:4], None)

            def branch_b(L):
                for h in range(H):
                    evac_gain([(qk_t[:, 0:T], 0, T, None, P), (qk_t[:, T:2 * T], T, 2 * T, None, P)])
                    yield
                    ps.take()
                    yield
                    squares_of_output()
                    yield
                    tail(12 + h, ret_gain[:, h:h + 1])
                    yield

            def squares_of_x(xs=xs, xn=xn):
                n = xsq.take()
                act.wait_ge(x_ready, xsq.value(n + 1))
                for t in range(TT):
                    last = nc.scalar.activation(xn[:, t, :], xs[:, t, :], ACT.Square, accum_out=x_ssq[:, t:t + 1])
                last.then_inc(x_sq_done, 1)

            for a, b in ((ident[:], k_ident), (ret_tab[:], k_ret), (tmp[:, 0:LEVELS * P], k_levels),
                         (seen[:].rearrange("p t s -> p (t s)"), k_seen),
                         (cos[:].rearrange("p t n -> p (t n)"), k_cos), (sin[:].rearrange("p t n -> p (t n)"), k_sin),
                         (k2[:, 0].rearrange("p t n -> p (t n)"), k_cos2), (k2[:, 1].rearrange("p t n -> p (t n)"), k_sin2)):
                act.dma_start(a, b).then_inc(consts_in, 16)
            columns = []
            for l in range(DEPTH):
                columns += [(par_l[:, l, 0:16], norm_g[l].rearrange("(k p) -> p k", p=P)), (par_l[:, l, 16:20], qk_g[l].rearrange("j p -> p j")),
                            (par_l[:, l, 20:24], ret_g[l].rearrange("h p -> p h")), (par_l[:, l, 24:28], hgrn_g[l].rearrange("h p -> p h")),
                            (lg[:, l, :], lb_logits[l].rearrange("h p -> p h"))]
            columns += [(p_mix, g_mix[0].rearrange("(k p) -> p k", p=P)), (p_ffn, g_ffn[0].rearrange("(k p) -> p k", p=P)),
                        (p_cq, g_cq[0].rearrange("(k p) -> p k", p=P)), (p_ckv, g_ckv[0].rearrange("(k p) -> p k", p=P))]
            columns += [(p_h2[:, i:i + 1], g.rearrange("l p -> p l")) for i, g in enumerate((g_qn, g_kn, g_qd, g_kd))]
            columns += [(g2[:, i, :], g.partition_broadcast(P).rearrange("p l n -> p (l n)")) for i, g in enumerate((g_qr, g_kr))]
            assert len(columns) == N_PARS
            with nc.allow_non_contiguous_dma(reason="parameters as columns, a few kilobytes"):
                for a, b in columns:
                    act.dma_start(a, b).then_inc(pars_in, 16)
            act.wait_ge(lb_shifted, 1)
            nc.scalar.activation(le[:], lg[:], ACT.Exp).then_inc(lb_exp, 1)
            feed(KD, xh, 0)
            prev = blocks([("copy", area(Q0 + 1024 * i, 0, NB), KD, NB) for i in range(PRO_BLOCKS)])
            finish(prev)
            act.wait_ge(mkv_out, 16)

            def layer(L):
                squares_of_x()
                act.wait_ge(pars_now, xsq.value(xsq.k))
                feed(KD, xh, 0, lambda k: x_gain[:, k:k + 1])
                act.wait_ge(x_out, xsq.round_value(xsq.k - 1, 16) + 16)

                def attention():
                    yield from branch_c(L)
                    yield from branch_a(L)
                    yield from branch_m(L)
                    yield from branch_b(L)

                side = attention()
                y = [0]

                def phase():
                    y[0] += 1
                    for _ in range(phases_after(y[0])):
                        next(side)

                prev = blocks([(k, u[name], KD, width) for name, col, width, k in IN_BLOCKS], phase=phase)
                finish(blocks([("sigmoid", sig, KD, NB), ("merge", None, 4, NB)] * 4, prev, phase))
                for _ in side:
                    pass

                def gate_pair(i):
                    finish(blocks([("sigmoid", sig, KD, NB), ("merge", None, 4, NB)] * 6))

                repeat(act, 2, [(ch, 60), (bl, 12), (gu, 6)], gate_pair)
                feed(KD, xh, 0)
                blocks([("add", None, KD, NB)] * 4)

            repeat(act, DEPTH, [(ch, LAYER_CHUNKS), (bl, LAYER_BLOCKS), (pt, PT_LAYER), (ps, PS_LAYER), (po, 16), (gu, 16), (smx, 8),
                                (xsq, 1), (ru, 8)], layer, "act layer")

            squares_of_x()
            feed(KD, xh, 0, lambda k: p_mix[:, k:k + 1])
            act.wait_ge(x_out, 16 * (DEPTH + 1))

            def latent_squares():
                for i, src in enumerate((cqn, ckvn)):
                    b = LAST_BLOCK[("cq", "ckv")[i]]
                    act.wait_ge(gm_free[b % 2], b // 2 + 1)
                    for t in range(TT):
                        last = nc.scalar.activation(tmp[:, 1024 + 1024 * i:2048 + 1024 * i].rearrange("p (t n) -> p t n", t=TT)[:, t, :], src[:, t, :], ACT.Square, accum_out=x_ssq[:, 2 * i + t:2 * i + t + 1])
                last.then_inc(x_sq_done, 1)

            def dilated():
                for _ in range(4):
                    yield
                for h in range(HEADS2):
                    yield from soft(h, 1.0, p_h2[:, 2:3], p_h2[:, 3:4], sc)

            def attention2():
                yield from woven(dilated(), dict(zip(LATENT_PHASES, (latent_squares, nothing, lambda: feed(4, yh, 8, lambda k: p_cq[:, k:k + 1]),
                                                                     lambda: feed(4, yh, 12, lambda k: p_ckv[:, k:k + 1])))))
                for _ in range(6):
                    yield
                evac_gain([(kr_t, 0, T, None, ROPE2)])
                yield
                for h in range(HEADS2):
                    yield from soft(8 + h, QW ** -0.5, p_h2[:, 0:1], p_h2[:, 1:2], None, extra=True)

            side = attention2()
            y2 = [0]

            def phase2():
                y2[0] += 1
                for _ in range(phases2_by(y2[0]) - phases2_by(y2[0] - 1)):
                    next(side)

            prev = blocks([(k, u[name], KD, width) for name, col, width, k in IN2_BLOCKS], phase=phase2)
            prev = blocks([(k, u[name], 4, width) for name, col, width, k in UQ_BLOCKS + UKV_BLOCKS], prev, phase2)
            finish(blocks([("bias", None, KD, NB), ("merge", None, 8, NB)] * 4, prev, phase2))
            for _ in side:
                pass

            def gate2_block(n):
                finish(blocks([("bias", None, KD, NB), ("merge", None, 8, NB)]))

            repeat(act, 4, [(ch, 12), (bl, 2)], gate2_block)
            gu.k += 8
            feed(KD, xh, 0)
            blocks([("add", None, KD, NB)] * 4)
            squares_of_x(xs2, merged2)
            feed(KD, xh, 0, lambda k: p_ffn[:, k:k + 1])
            blocks([("gate", sig, KD, NB), ("up", None, KD, NB)])

            def ffn(i):
                gate = (bl.take(), ch.k + 8, "gate", sig, NB)
                for s in range(8):
                    split()
                for n in range(4):
                    bl.take()
                    for s in range(2):
                        split()
                        if (n, s) == (0, 0):
                            feed(4, yh, 0)
                        if (n, s) == (1, 1):
                            read_out(*gate)
                bl.take()
                for s in range(8):
                    split()

            repeat(act, N_FF - 1, [(ch, 24), (bl, 6), (pt, 2), (gu, 1)], ffn)
            feed(4, yh, 0)
            for n in range(4):
                for s in range(2):
                    split()

        @block.vector
        def _(dve):
            ch, bl = Tally(RING), Tally(2)
            pt, ps, po = Tally(2), Tally(), Tally()
            sg, smx, xr, hi, osc, yr, hs, ru, idx, chain = (Tally() for _ in range(10))
            V = nc.vector

            def link(ins):
                ins.then_inc(dve_chain, 1)
                hold(dve, dve_chain, chain.value(chain.take() + 1))

            def split(width=NB):
                c = ch.take()
                dve.wait_ge(hi_done, ch.value(c + 1))
                if c >= RING:
                    dve.wait_ge(mm_done, ch.value(c - RING + 1))
                V.tensor_tensor(w_lo[:, c % RING, :, 0:width], raw[:, c % RING, :, 0:width],
                                w_hi[:, c % RING, :, 0:width].bitcast(F32), ALU.subtract).then_inc(lo_done, 1)

            with_bias = False

            def read_out(b, c_end, kind, dst, width=NB):
                g = G[b % 2][:, :, 0:width]
                if kind in ("silu", "gate"):
                    dve.wait_ge(sig_done, sg.value(sg.take() + 1))
                elif kind in ("merge", "merge0", "up", "add", "bias"):
                    dve.wait_ge(mm_done, ch.value(c_end))
                if kind == "silu":
                    V.tensor_tensor(dst, g, dst, ALU.mult).then_inc(gm_free[b % 2], 1)
                elif kind == "gate":
                    V.tensor_tensor(dst, g, sig, ALU.mult).then_inc(gm_free[b % 2], 1)
                    dve.wait_ge(gm_free[b % 2], bl.round_value(b) + 1)
                    dve.sem_inc(sig_used, 1)
                elif kind == "up":
                    V.tensor_tensor(dst, g, dst, ALU.mult).then_inc(gm_free[b % 2], 1)
                    dve.wait_ge(gm_free[b % 2], bl.round_value(b) + 1)
                    dve.sem_inc(ffn_ready, 1)
                elif kind == "add":
                    V.tensor_tensor(dst, g, dst, ALU.add).then_inc(gm_free[b % 2], 1)
                elif kind == "bias":
                    if bl.rounds is None:
                        dve.wait_ge(bias_in[1], 16)
                    V.tensor_tensor(sig, g, dst, ALU.add).then_inc(gm_free[b % 2], 1)
                elif kind in ("merge", "merge0"):
                    if with_bias:
                        dve.wait_ge(sig_done, sg.value(sg.take() + 1))
                    else:
                        dve.wait_ge(gm_free[(b - 1) % 2], bl.round_value(b - 1) + 1)
                    V.tensor_tensor(sig, g, sig, ALU.mult).then_inc(gm_free[b % 2], 1)
                    dve.wait_ge(gm_free[b % 2], bl.round_value(b) + 1)
                    if kind == "merge0":
                        V.tensor_copy(dst, sig).then_inc(sig_used, 1)
                    else:
                        V.tensor_tensor(dst, sig, dst, ALU.add).then_inc(sig_used, 1)

            def blocks(items, left=(), phase=None):
                left = list(left)
                for kind, dst, kt, width in items:
                    b = bl.take()
                    for s in range(kt // CK):
                        split(width)
                        if left and left[0][1] + RING == ch.k:
                            read_out(*left.pop(0))
                        if phase:
                            phase()
                    left.append((b, ch.k, kind, dst, width))
                return left

            def finish(left):
                for block_left in left:
                    read_out(*block_left)
                return left[-1][0]

            def low(pieces):
                i, n = pt.take(), hi.take()
                dve.wait_ge(pt_hi, hi.value(n + 1))
                for h, l, a, b, gain in pieces:
                    z = PT[i % 2][:, a:b]
                    if gain is None:
                        if h.ndim == 3:
                            z = z.rearrange("p (k t) -> p k t", t=T)
                        last = V.tensor_tensor(l, z, h.bitcast(F32), ALU.subtract)
                    else:
                        last = V.scalar_tensor_tensor(out=l, in0=z, scalar=gain, in1=h.bitcast(F32), op0=ALU.mult, op1=ALU.subtract)
                last.then_inc(pt_free[i % 2], 1)

            def feed(kt, h, l, kk, gain=None):
                for k in range(0, kt, 2):
                    if gain is None:
                        a = slice(kk + k, kk + k + 2)
                        low([(h[:, a, :], l[:, a, :], 0, 512, None)])
                    else:
                        low([(h[:, kk + k + j, :], l[:, kk + k + j, :], j * T, (j + 1) * T, gain(k + j)) for j in range(2)])

            def gated(z, scale_of_row):
                o, r = po.take(), yr.take()
                dve.wait_ge(po_full, po.value(o + 1))
                for t in range(TT):
                    last = V.scalar_tensor_tensor(out=yz[:, r % 2, t, :], in0=PO[:, t * P:(t + 1) * P], scalar=scale_of_row[:, t:t + 1],
                                                  in1=z(t), op0=ALU.mult, op1=ALU.mult)
                last.then_inc(y_ready, 1)

            def ungated(scale_of_row):
                o, r = po.take(), yr.take()
                dve.wait_ge(po_full, po.value(o + 1))
                for t in range(TT):
                    last = V.tensor_scalar(yz[:, r % 2, t, :], PO[:, t * P:(t + 1) * P], scale_of_row[:, t:t + 1], None, ALU.mult)
                last.then_inc(y_ready, 1)

            def normed(z):
                n = osc.take()
                dve.wait_ge(o_scaled, osc.value(n + 1))
                gated(z, o_rs)

            def tail(kk, gain):
                low([(yh[:, kk, :], yl[:, kk, :], 0, T, gain)])

            def soft(kk, scale, z, bias=None, slope=None, rotated=False):
                pt.take()
                if rotated:
                    pt.take()
                yield
                s, e = ps.take(), smx.take()
                dve.wait_ge(ps_full, ps.value(s + 1))
                flat = sc.rearrange("p t s -> p (t s)")
                src = sc
                if slope is not None:
                    link(V.scalar_tensor_tensor(out=flat, in0=PS[:], scalar=HD ** -0.5, in1=ret_tab[:, 512:1024], op0=ALU.mult, op1=ALU.add))
                    V.scalar_tensor_tensor(out=flat, in0=ret_tab[:, 0:512], scalar=slope, in1=flat, op0=ALU.mult, op1=ALU.add).then_inc(ps_free, 1)
                    dve.wait_ge(ps_free, ps.value(s + 2))
                elif bias is not None:
                    V.tensor_tensor(flat, PS[:], bias, ALU.add).then_inc(ps_free, 1)
                    dve.wait_ge(ps_free, ps.value(s + 2))
                else:
                    src = PS[:].rearrange("p (t s) -> p t s", t=TT)
                link(V.reduce_max(mx, src, AX))
                V.tensor_scalar(nmx, mx, -scale, None, ALU.mult).then_inc(max_done, 1)
                yield
                dve.wait_ge(exp_done, smx.value(e + 1))
                r = V.reciprocal(r_e, esum)
                if src is sc:
                    link(r)
                else:
                    r.then_inc(ps_free, 1)
                i = pt.take()
                dve.wait_ge(pt_full, pt.value(i + 1))
                V.tensor_copy(p_t.rearrange("p s t -> p (s t)"), PT[i % 2][:]).then_inc(pt_free[i % 2], 1)
                yield
                if z is None:
                    ungated(r_e)
                else:
                    gated(z, r_e)
                yield
                tail(kk, None)
                yield

            def sum_heads(size=1024, width=P):
                n = hs.take()
                dve.wait_ge(heads_squared, hs.value(n + 1))
                V.reduce_sum(ssq[:, 0:size // width], squares[:, 0:size].rearrange("p (h n) -> p h n", n=width), AX).then_inc(heads_summed, 1)

            def hd(z, h):
                return lambda t: z[:, t, h * P:(h + 1) * P]

            def branch_c():
                for g in range(2):
                    i = pt.take()
                    turns_read(dve, pt, i, both=False)
                    for j in range(2):
                        h = 2 * g + j
                        last = V.tensor_scalar(f2[:, j * T:(j + 1) * T], f2[:, j * T:(j + 1) * T], oml[:, h:h + 1], lb[:, h:h + 1], ALU.mult, ALU.add)
                    link(last)
                    for a, b in zip(prod[:-1], prod[1:]):
                        e = a.rearrange("p (n two) -> p n two", two=2)
                        last = V.tensor_tensor(b, e[:, :, 0], e[:, :, 1], ALU.mult)
                        if b is not prod[-1]:
                            link(last)
                    last.then_inc(gates_ready, 1)
                    yield
                    i = pt.take()
                    turns_read(dve, pt, i, both=False)
                    V.tensor_tensor(qp[0], q_c, f2, ALU.mult).then_inc(qp_ready, 1)
                    link(V.memset(acc, 0.0))
                    yield
                    for l in range(LEVELS + 1):
                        if 1 <= l < LEVELS:
                            m = HALVES[l - 1]
                            old = qp_buf(l).rearrange("p (n two m) -> p n two m", two=2, m=m)
                            new = qp_buf(l + 1).rearrange("p (n two m) -> p n two m", two=2, m=m)
                            left = prod[l - 1].rearrange("p (n two) -> p n two", two=2)[:, :, 0].unsqueeze(2).broadcast_to([P, 256 // m, m])
                            V.tensor_copy(new[:, :, 0, :], old[:, :, 0, :])
                            V.tensor_tensor(new[:, :, 1, :], old[:, :, 1, :], left, ALU.mult).then_inc(qp_ready, 1)
                        s = ps.take()
                        hold(dve, ps_full, ps.value(s + 1))
                        if l < LEVELS:
                            mask = levels[:, l, :].unsqueeze(1).broadcast_to([P, 4, P])
                            V.copy_predicated(acc.rearrange("p (a t) -> p a t", t=P), mask, PS[:].rearrange("p (a t) -> p a t", t=P)).then_inc(ps_free, 1)
                            dve.wait_ge(ps_free, ps.value(s + 2))
                        else:
                            V.tensor_copy(acc_off, PS[:, 0:2 * P]).then_inc(ps_free, 1)
                            dve.wait_ge(ps_free, ps.value(s + 2))
                            dve.sem_inc(acc_ready, 1)
                        yield
                    for j in range(2):
                        normed(hd(u["c_z"], 2 * g + j))
                        yield
                        tail(2 * g + j, hg_gain[:, 2 * g + j:2 * g + j + 1])
                        yield

            def branch_a():
                sum_heads()
                yield
                sum_heads()
                yield
                pt.take()
                pt.take()
                n = idx.take()
                dve.wait_ge(idx_ready, idx.value(n + 1))
                link(V.tensor_copy(score, seen[:]))
                yield
                for h in range(0, IDX_HEADS, 2):
                    pt.take()
                    yield
                for t in range(TT):
                    for h in range(0, IDX_HEADS, 2):
                        s = ps.take()
                        n = ru.take()
                        dve.wait_ge(ps_free, ps.value(s + 2))
                        for j in range(2):
                            ins = V.scalar_tensor_tensor(out=score[:, t, :], in0=rel[(s - PS_C) % 2][:, j * T:(j + 1) * T], scalar=wis[:, t, h + j:h + j + 1],
                                                         in1=score[:, t, :], op0=ALU.mult, op1=ALU.add)
                            if j == 0:
                                link(ins)
                        ins.then_inc(rel_used, 1)
                        hold(dve, rel_used, ru.value(n + 3))
                        yield
                for r in range(N_SEL // 8):
                    for t in range(TT):
                        top = top8[:, 8 * t:8 * t + 8]
                        link(V.max(top, score[:, t, :]))
                        link(V.match_replace(score[:, t, :], top, score[:, t, :], -3e38))
                    if r == N_SEL // 8 - 1:
                        link(V.tensor_scalar(score, score, -2e38, -BIG, ALU.is_gt, ALU.mult))
                    yield
                for h in range(H):
                    yield from soft(4 + h, HD ** -0.5, hd(u["a_z"], h), bias=score.rearrange("p t s -> p (t s)"))

            def branch_m():
                sum_heads()
                yield
                sum_heads()
                yield
                for h in range(H):
                    yield from soft(8 + h, HD ** -0.5, hd(u["m_z"], h))

            def branch_b():
                for h in range(H):
                    pt.take()
                    yield
                    s = ps.take()
                    dve.wait_ge(ps_full, ps.value(s + 1))
                    V.tensor_tensor(p_t.rearrange("p s t -> p (s t)"), PS[:], ret_tab[:, h * 512:(h + 1) * 512], ALU.mult).then_inc(ps_free, 1)
                    dve.wait_ge(ps_free, ps.value(s + 2))
                    dve.sem_inc(decayed, 1)
                    yield
                    normed(hd(u["b_z"], h))
                    yield
                    tail(12 + h, ret_gain[:, h:h + 1])
                    yield

            def normalize_x(xs=xs, xn=xn):
                n = xr.take()
                dve.wait_ge(x_rs_done, xr.value(n + 1))
                for t in range(TT):
                    last = V.tensor_scalar(xn[:, t, :], xs[:, t, :], x_rs[:, t:t + 1], None, ALU.mult)
                last.then_inc(xn_done, 1)

            dve.sem_inc(ps_free, 1)
            dve.sem_inc(y_ready, 1)
            dve.sem_inc(sig_used, 1)
            dve.sem_inc(rel_used, 2)
            dve.wait_ge(consts_in, CONSTS_IN)
            link(V.tensor_copy(levels[:].rearrange("p l q -> p (l q)"), tmp[:, 0:LEVELS * P]))
            dve.wait_ge(pars_in, PARS_IN)
            link(V.tensor_tensor(lt[:, 0, :], lg[:, 0, :], lg[:, 1, :], ALU.max))
            V.tensor_tensor(lg[:, 0, :], lg[:, 0, :], lt[:, 0, :], ALU.subtract)
            V.tensor_tensor(lg[:, 1, :], lg[:, 1, :], lt[:, 0, :], ALU.subtract).then_inc(lb_shifted, 1)
            dve.wait_ge(lb_exp, 1)
            link(V.tensor_tensor(lt[:, 0, :], le[:, 0, :], le[:, 1, :], ALU.add))
            link(V.reciprocal(lt[:, 1, :], lt[:, 0, :]))
            for l in range(DEPTH):
                link(V.tensor_tensor(le[:, l, :], le[:, l, :], lt[:, 1, :], ALU.mult))
            V.tensor_tensor(par_l[:, 0, 28:32], le[:, 0, :], le[:, 0, :], ALU.subtract)
            link(V.tensor_tensor(lt[:, 0, :], le[:, 0, :], le[:, 1, :], ALU.add))
            link(V.tensor_tensor(par_l[:, 1, 28:32], lt[:, 0, :], le[:, 0, :], ALU.subtract))
            for l in range(DEPTH):
                link(V.tensor_scalar(par_l[:, l, 32:36], par_l[:, l, 28:32], -1.0, 1.0, ALU.mult, ALU.add))
            feed(KD, xh, xl, 0)
            blocks([("copy", None, KD, NB)] * PRO_BLOCKS)
            dve.wait_ge(x_in, 16)
            dve.sem_inc(x_ready, 1)

            def layer(L):
                V.tensor_copy(now, par_l[:, bass.ds(L, 1), :].rearrange("p l n -> p (l n)")).then_inc(pars_now, 1)
                n = xr.k
                dve.wait_ge(pars_now, xr.value(n + 1))
                normalize_x()
                feed(KD, xh, xl, 0, lambda k: x_gain[:, k:k + 1])

                def attention():
                    yield from branch_c()
                    yield from branch_a()
                    yield from branch_m()
                    yield from branch_b()

                side = attention()
                y = [0]

                def phase():
                    y[0] += 1
                    for _ in range(phases_after(y[0])):
                        next(side)

                prev = blocks([(k, u[name], KD, width) for name, col, width, k in IN_BLOCKS], phase=phase)
                items = []
                for n in range(4):
                    items += [("sigmoid", None, KD, NB), ("merge0", merged[:, :, n * NB:(n + 1) * NB], 4, NB)]
                finish(blocks(items, prev, phase))
                for _ in side:
                    pass

                def gate_pair(i):
                    items = []
                    for n in range(2):
                        items += [("sigmoid", None, KD, NB), ("merge", merged[:, :, bass.ds(i * 2 * NB + n * NB, NB)], 4, NB)] * 3
                    finish(blocks(items))

                repeat(dve, 2, [(ch, 60), (bl, 12)], gate_pair)
                feed(KD, xh, xl, 0)
                dve.wait_ge(x_back, xr.round_value(xr.k, 16))
                prev = blocks([("add", xs[:, :, i * NB:(i + 1) * NB], KD, NB) for i in range(4)])
                last = finish(prev)
                dve.wait_ge(gm_free[last % 2], bl.round_value(last) + 1)
                dve.sem_inc(x_ready, 1)

            repeat(dve, DEPTH, [(ch, LAYER_CHUNKS), (bl, LAYER_BLOCKS), (pt, PT_LAYER), (hi, 16 + 16), (ps, PS_LAYER), (po, 16), (yr, 16), (sg, 4),
                                (smx, 8), (xr, 1), (osc, 8), (hs, 4), (ru, 8), (idx, 1), (chain, CHAIN["dve"])], layer, "dve layer")

            normalize_x()
            feed(KD, xh, xl, 0, lambda k: p_mix[:, k:k + 1])

            def latent_scale():
                n = xr.take()
                dve.wait_ge(x_rs_done, xr.value(n + 1))
                for i, src in enumerate((cqn, ckvn)):
                    for t in range(TT):
                        last = V.tensor_scalar(src[:, t, :], src[:, t, :], x_rs[:, 2 * i + t:2 * i + t + 1], None, ALU.mult)
                last.then_inc(xn_done, 1)

            def dilated():
                for _ in range(4):
                    sum_heads()
                    yield
                dve.wait_ge(dil_in, 16)
                for h in range(HEADS2):
                    yield from soft(h, 1.0, None, slope=2.0 ** -(h + 1))

            def attention2():
                yield from woven(dilated(), dict(zip(LATENT_PHASES, (nothing, latent_scale, lambda: feed(4, yh, yl, 8, lambda k: p_cq[:, k:k + 1]),
                                                                     lambda: feed(4, yh, yl, 12, lambda k: p_ckv[:, k:k + 1])))))
                for size, width in ((TT * ROPE2, ROPE2), (1024, P), (1024, P), (1024, ROPE2), (1024, P), (1024, P)):
                    sum_heads(size, width)
                    yield
                pt.take()
                yield
                for h in range(HEADS2):
                    yield from soft(8 + h, QW ** -0.5, None, rotated=True)

            side = attention2()
            y2 = [0]

            def phase2():
                y2[0] += 1
                for _ in range(phases2_by(y2[0]) - phases2_by(y2[0] - 1)):
                    next(side)

            prev = blocks([(k, u[name], KD, width) for name, col, width, k in IN2_BLOCKS], phase=phase2)
            prev = blocks([(k, u[name], 4, width) for name, col, width, k in UQ_BLOCKS + UKV_BLOCKS], prev, phase2)
            with_bias = True
            items = []
            for n in range(4):
                row = bias_rows[1][:, n * NB:(n + 1) * NB].unsqueeze(1).broadcast_to([P, TT, NB])
                items += [("bias", row, KD, NB), ("merge0", merged2[:, :, n * NB:(n + 1) * NB], 8, NB)]
            finish(blocks(items, prev, phase2))
            for _ in side:
                pass
            dve.wait_ge(bias_in[0], 16)

            def gate2_block(n):
                row = bias_rows[0][:, bass.ds(n * NB, NB)].unsqueeze(1).broadcast_to([P, TT, NB])
                finish(blocks([("bias", row, KD, NB), ("merge", merged2[:, :, bass.ds(n * NB, NB)], 8, NB)]))

            repeat(dve, 4, [(ch, 12), (bl, 2), (sg, 1)], gate2_block)
            feed(KD, xh, xl, 0)
            dve.wait_ge(x_back, 16 * (DEPTH + 1))
            prev = blocks([("add", xs2[:, :, i * NB:(i + 1) * NB], KD, NB) for i in range(4)])
            last = finish(prev)
            dve.wait_ge(gm_free[last % 2], bl.round_value(last) + 1)
            dve.sem_inc(x_ready, 1)
            normalize_x(xs2, merged2)
            feed(KD, xh, xl, 0, lambda k: p_ffn[:, k:k + 1])
            blocks([("gate", hidden, KD, NB), ("up", hidden, KD, NB)])

            def ffn(i):
                up_before = (bl.k - 1, ch.k, "up", hidden, NB)
                gate = (bl.take(), ch.k + 8, "gate", hidden, NB)
                for s in range(8):
                    split()
                    if s == 3:
                        read_out(*up_before)
                downs = []
                for n in range(4):
                    b = bl.take()
                    for s in range(2):
                        split()
                        if (n, s) == (0, 0):
                            feed(4, yh, yl, 0)
                        if (n, s) == (1, 1):
                            read_out(*gate)
                        if s == 1 and n >= 2:
                            read_out(*downs[n - 2])
                    downs.append((b, ch.k, "add", xs2[:, :, n * NB:(n + 1) * NB], NB))
                bl.take()
                for s in range(8):
                    split()
                    if s in (1, 3):
                        read_out(*downs[2 + s // 2])

            repeat(dve, N_FF - 1, [(ch, 24), (bl, 6), (pt, 2), (hi, 2), (sg, 1)], ffn)
            read_out(bl.k - 1, ch.k, "up", hidden, NB)
            feed(4, yh, yl, 0)
            prev = blocks([("add", xs2[:, :, n * NB:(n + 1) * NB], 4, NB) for n in range(4)])
            last = finish(prev)
            dve.wait_ge(gm_free[last % 2], bl.round_value(last) + 1)
            dve.sem_inc(x_ready, 1)

        @block.gpsimd
        def _(pool):
            bl, xe, lyr = Tally(2), Tally(), Tally()
            pt, ps, lvl, hs, osq, pair, rel0, chain = Tally(2), Tally(), Tally(), Tally(), Tally(), Tally(), Tally(), Tally()
            V = nc.gpsimd

            def link(ins):
                ins.then_inc(pool_chain, 1)
                hold(pool, pool_chain, chain.value(chain.take() + 1))

            def evacuated(name, table):
                b = table[name]
                hold(pool, gm_free[b % 2], bl.round_value(b) + 1)

            def root(dst, src, count, n):
                link(V.tensor_scalar(src, src, 1.0 / count, EPS, ALU.mult, ALU.add))
                return V.tensor_tensor(dst, src, half[:, 0:n], ALU.pow)

            def x_norm(count=D, n=TT):
                e = xe.take()
                hold(pool, x_sq_done, xe.value(e + 1))
                root(x_rs[:, 0:n], x_ssq[:, 0:n], count, n).then_inc(x_rs_done, 1)

            def head_norm(views, heads, width=P):
                n = hs.take()
                size = TT * heads * width
                sq = squares[:, 0:size].rearrange("p (t h n) -> p t h n", t=TT, n=width)
                V.tensor_tensor(sq, views, views, ALU.mult).then_inc(heads_squared, 1)
                hold(pool, heads_summed, hs.value(n + 1))
                g = TT * heads
                link(root(rs[:, 0:g], ssq[:, 0:g], width, g))
                by = rs[:, 0:g].rearrange("p (t h) -> p t h", t=TT).unsqueeze(3).broadcast_to([P, TT, heads, width])
                ins = V.tensor_tensor(views, views, by, ALU.mult)
                return ins

            def split_heads(z, n=P):
                return z.rearrange("p t (h n) -> p t h n", n=n)

            def output_norms(n):
                for _ in range(n):
                    o = osq.take()
                    hold(pool, o_squared, osq.value(o + 1))
                    root(o_rs, o_ssq, HD, TT).then_inc(o_scaled, 1)

            def branch_c():
                for g in range(2):
                    n = pair.take()
                    hold(pool, gates_ready, pair.value(n + 1))
                    V.tensor_scalar(ks[0], f2, -1.0, 1.0, ALU.mult, ALU.add).then_inc(ks_ready, 1)
                    n = lvl.take()
                    first = ps.k
                    for l in range(1, LEVELS):
                        m = HALVES[l - 1]
                        hold(pool, ks_ready, lvl.value(lvl.k))
                        hold(pool, ps_full, ps.value(first + l))
                        old = ks_buf(l).rearrange("p (n two m) -> p n two m", two=2, m=m)
                        new = ks_buf(l + 1).rearrange("p (n two m) -> p n two m", two=2, m=m)
                        right = prod[l - 1].rearrange("p (n two) -> p n two", two=2)[:, :, 1].unsqueeze(2).broadcast_to([P, 256 // m, m])
                        V.tensor_copy(new[:, :, 1, :], old[:, :, 1, :])
                        V.tensor_tensor(new[:, :, 0, :], old[:, :, 0, :], right, ALU.mult).then_inc(ks_ready, 1)
                        lvl.take()
                    ps.k += LEVELS + 1
                    output_norms(2)

            def rotate(z, heads, n, c_s):
                a, b, d = (r[:, 0:TT * heads * n].rearrange("p (t h n) -> p t h n", t=TT, h=heads) for r in rope_t)
                x1, x2 = z[:, :, :, 0:n], z[:, :, :, n:2 * n]
                c1, s2, s1, c2 = (w.unsqueeze(2).broadcast_to([P, TT, heads, n]) for w in c_s)
                V.tensor_tensor(a, x1, c1, ALU.mult)
                V.tensor_tensor(b, x2, s2, ALU.mult)
                link(V.tensor_tensor(d, x1, s1, ALU.mult))
                link(V.tensor_tensor(x2, x2, c2, ALU.mult))
                V.tensor_tensor(x1, a, b, ALU.subtract)
                return V.tensor_tensor(x2, x2, d, ALU.add)

            pool.dma_start(xs, rows(mem[0])).then_inc(mem_in, 16)
            link(V.memset(half, -0.5))
            hold(pool, pt_full, KD // 2)
            pool.dma_start(xs, rows(x[0])).then_inc(x_in, 16)
            for q in range(2):
                hold(pool, gm_free[q], PRO_BLOCKS // 2)
            pool.dma_start(mkv_kept.rearrange("i (t p) n -> p (i t) n", p=P),
                           arena[:, Q0:Q0 + 4096].rearrange("p (i n) -> p i n", n=NB)).then_inc(mkv_out, 16)
            hold(pool, mkv_out, 16)

            def layer(L):
                n = lyr.take()
                hold(pool, x_ready, lyr.value(n + 1))
                pool.dma_start(rows(x_kept), xs).then_inc(x_out, 16)
                pool.dma_start(arena[:, M_0:M_0 + 2048].rearrange("p (i n) -> p i n", n=NB),
                               mkv_kept.rearrange("(l i) (t p) n -> l p (i t) n", l=DEPTH, p=P)[bass.ds(L, 1)][0]).then_inc(mkv_in, 16)
                x_norm()
                branch_c()
                turns_read(pool, pt, 8 + PT_C - 1, wait=hold)
                for name in ("a_q", "a_k"):
                    evacuated(name, LAYER_BLOCK)
                    head_norm(split_heads(u[name]), H).then_inc(heads_normed, 1)
                evacuated("a_kw", LAYER_BLOCK)
                hold(pool, heads_normed, hs.value(hs.k))
                V.tensor_scalar(wis, u["a_kw"][:, :, IDX_DIM:], IDX_HEADS ** -0.5 * IDX_DIM ** -0.5, None, ALU.mult).then_inc(idx_ready, 1)
                hold(pool, ps_full, ps0.value(PS_SEL))
                hold(pool, mkv_in, lyr.round_value(n, 16) + 16)
                evacuated("m_q", LAYER_BLOCK)
                head_norm(split_heads(u["m_q"]), H).then_inc(heads_normed, 1)
                head_norm(split_heads(mk), H).then_inc(heads_normed, 1)
                evacuated("b_q", LAYER_BLOCK)
                evacuated("b_k", LAYER_BLOCK)
                for i, name in enumerate(("b_q", "b_k")):
                    ins = rotate(split_heads(u[name]), H, 64, (cos[:], sin[:], sin[:], cos[:]))
                    if i:
                        ins.then_inc(roped, 1)
                    else:
                        link(ins)
                output_norms(4)
                turns_read(pool, pt, 8 + PT_ATT - 1, wait=hold)
                hold(pool, x_out, lyr.round_value(n, 16) + 16)
                pool.dma_start(xs, rows(x_kept)).then_inc(x_back, 16)
                pt.k += PT_LAYER
                ps0.k += PS_LAYER
                ps.k += PS_LAYER - PS_C
                bl.k += LAYER_BLOCKS

            ps0 = Tally()
            repeat(pool, DEPTH, [(bl, LAYER_BLOCKS), (pt, PT_LAYER), (ps, PS_LAYER), (ps0, PS_LAYER), (lyr, 1), (xe, 1), (pair, 2), (lvl, 2 * LEVELS),
                                 (hs, 4), (osq, 8), (chain, CHAIN["pool"])], layer, "pool layer")

            hold(pool, x_ready, DEPTH + 1)
            pool.dma_start(rows(x_kept), xs).then_inc(x_out, 16)
            pool.dma_start(ret_tab[:, 0:1024], k_dil).then_inc(dil_in, 16)
            x_norm()
            bl.k = 0
            for name, z in (("qd1", qd), ("kd1", kd)):
                evacuated(name[:-1] + "0", LAST_BLOCK)
                evacuated(name, LAST_BLOCK)
                for i in range(2):
                    head_norm(split_heads(z[:, :, i * NB:(i + 1) * NB]), 4).then_inc(heads_normed, 1)
            hold(pool, heads_normed, hs.value(hs.k))
            for q in range(2):
                for k, (j, f) in enumerate(((0, 0), (1, 1), (0, 1), (1, 0))):
                    gain = g2[:, q, 32 * j:32 * j + 32].unsqueeze(1).broadcast_to([P, TT, 32])
                    last = V.tensor_tensor(rope2_tab[:, q, k], k2[:, f], gain, ALU.mult)
            link(last)
            x_norm(NB, 4)
            turns_read(pool, pt, PT_DIL - 1, wait=hold)
            pool.dma_start(bias_rows[1], b_gate[:, D:2 * D].partition_broadcast(P).rearrange("p l n -> p (l n)")).then_inc(bias_in[1], 16)
            for i in range(3):
                evacuated(f"uq{i}", LAST_BLOCK)
            for i in range(4):
                evacuated(f"ukv{i}", LAST_BLOCK)
            q_h = q2.rearrange("p t (h n) -> p t h n", n=QW)
            k_h = kv2.rearrange("p t (h n) -> p t h n", n=2 * P)
            kr_h = krn.rearrange("p t (h n) -> p t h n", h=1)
            for z, h, w in ((kr_h, 1, ROPE2), (q_h[:, :, 0:4, 0:NOPE], 4, P), (q_h[:, :, 4:8, 0:NOPE], 4, P), (q_h[:, :, :, NOPE:], 8, ROPE2),
                            (k_h[:, :, 0:4, 0:P], 4, P), (k_h[:, :, 4:8, 0:P], 4, P)):
                link(head_norm(z, h, w))
            tab = lambda q: tuple(rope2_tab[:, q, k] for k in range(4))
            link(rotate(q_h[:, :, :, NOPE:], HEADS2, 32, tab(0)))
            rotate(kr_h, 1, 32, tab(1)).then_inc(rope2_ready, 1)
            turns_read(pool, pt, PT_LAST - 1, wait=hold)
            pool.dma_start(bias_rows[0], b_gate[:, 0:D].partition_broadcast(P).rearrange("p l n -> p (l n)")).then_inc(bias_in[0], 16)
            pool.wait_ge(x_out, 16 * (DEPTH + 1))
            pool.wait_ge(sig_used, 16 * DEPTH + 4 + 1)
            pool.dma_start(xs2, rows(x_kept)).then_inc(x_back, 16)
            x_norm()
            pool.wait_ge(x_ready, DEPTH + 3)
            pool.dma_start(rows(out[0]), xs2).then_inc(all_out, 16)
            pool.wait_ge(all_out, 16)


N_PARS = 5 * DEPTH + 10
PARS_IN = 16 * N_PARS
CONSTS_IN = 16 * 8

INPUTS = ['x', 'mem', 'norm_g', 'w_in', 'qk_norm_g', 'ret_norm_g', 'hgrn_norm_g', 'lb_logits', 'w_mem_kv', 'w_branch', 'w_out',
          'g_mix_2', 'w_in_2', 'b_gate_2', 'g_cq_2', 'w_uq_2', 'g_ckv_2', 'w_ukv_2', 'g_q_nope_2', 'g_q_rope_2', 'g_k_nope_2',
          'g_k_rope_2', 'g_q_dil_2', 'g_k_dil_2', 'w_o_mla_2', 'w_o_dil_2', 'w_o_2', 'g_ffn_2', 'w_gate_up_2', 'w_down_2']


def kernel(**inputs):
    import concourse.bacc as bacc
    from concourse.bass_utils import run_bass_kernel_spmd

    nc = bacc.Bacc("TRN2", target_bir_lowering=False, num_devices=1)
    arrays = {f"in_{name}": np.ascontiguousarray(inputs[name]) for name in INPUTS}
    arrays |= {f"const_{name}": a for name, a in constants().items()}
    handles = {name: nc.dram_tensor(name, a.shape, mybir.dt.from_np(a.dtype), kind="ExternalInput").ap() for name, a in arrays.items()}
    x_kept = nc.dram_tensor("x_kept", (T, D), F32).ap()
    mkv_kept = nc.dram_tensor("mkv_kept", (2 * DEPTH, T, W), F32).ap()
    out = nc.dram_tensor("out", (1, T, D), F32, kind="ExternalOutput").ap()
    hybrid_program(nc, *handles.values(), x_kept, mkv_kept, out)
    got = run_bass_kernel_spmd(nc, [arrays], core_ids=[0])
    return got.results[0]["out"]
```
